# Optimizing a Trainium2 kernel written in Bass

```python
import math
import jax, jax.numpy as jnp
from jax import lax
import numpy as np

D_MODEL = 1024
BATCH = 1
SEQ = 1024
DEPTH = 1
DEC_BATCH = 8
DEC_SEQ = 1
PAST_LEN = 2048
PAGE_SIZE = 128

POOL_WIDTH = D_MODEL // 2
POOL_WINDOWS = (2, 4, 8, 16)
POOL_GROUPS = 4
POOL_GROUP_DIM = POOL_WIDTH // POOL_GROUPS
POOL_BUF = 15
N_HEADS = 8
N_KV_HEADS = 4
HEAD_DIM = 64
GROUP = N_HEADS // N_KV_HEADS
ATTN_WIDTH = N_HEADS * HEAD_DIM
KV_WIDTH = N_KV_HEADS * HEAD_DIM
IDX_HEADS = 4
IDX_DIM = 64
TOPK_MAX = 256
Q_BLOCK = 128
N_BUCKETS = 32
MAX_DISTANCE = 128
D_FF = -(-(8 * D_MODEL) // (3 * 256)) * 256
EPS = 1e-6
IN_SPLITS = (POOL_WIDTH, ATTN_WIDTH, KV_WIDTH, KV_WIDTH, IDX_HEADS * IDX_DIM, IDX_DIM, IDX_HEADS, 2 * D_MODEL)
IN_WIDTH = POOL_WIDTH + ATTN_WIDTH + 2 * KV_WIDTH + IDX_HEADS * IDX_DIM + IDX_DIM + IDX_HEADS + 2 * D_MODEL

kernel_name = 'hybrid_pool_dsa_decoder_step'

def rms_norm(x, g):
    xf = x.astype(jnp.float32)
    xf = xf * lax.rsqrt(jnp.mean(xf * xf, axis=-1, keepdims=True) + EPS)
    return xf.astype(x.dtype) * g

def project_in(x, ln1, w_in):
    B, S = x.shape[:2]
    z = jnp.einsum('bsd,de->bse', rms_norm(x, ln1), w_in)
    offs = np.cumsum((0,) + IN_SPLITS)
    u, q, k, v, qi, ki, wi, gates = [z[..., offs[i]:offs[i + 1]] for i in range(len(IN_SPLITS))]
    q = q.reshape(B, S, N_HEADS, HEAD_DIM)
    k = k.reshape(B, S, N_KV_HEADS, HEAD_DIM)
    v = v.reshape(B, S, N_KV_HEADS, HEAD_DIM)
    qi = qi.reshape(B, S, IDX_HEADS, IDX_DIM)
    return u, q, k, v, qi, ki, wi, gates

def pool_mixer(u_ext, n_prev, pos0, pool_w, pool_scale):
    T = u_ext.shape[1] - n_prev
    pos = pos0 + jnp.arange(T, dtype=jnp.int32)
    outs = []
    for gi, w in enumerate(POOL_WINDOWS):
        ug = u_ext[..., gi * POOL_GROUP_DIM:(gi + 1) * POOL_GROUP_DIM].astype(jnp.float32)
        cs = jnp.cumsum(ug, axis=1)
        lagged = jnp.pad(cs, ((0, 0), (w, 0), (0, 0)))[:, :cs.shape[1]]
        win = (cs - lagged)[:, n_prev:]
        count = jnp.minimum(w, pos + 1).astype(jnp.float32)
        d = win / count[None, :, None] - ug[:, n_prev:]
        outs.append(jnp.einsum('btc,ce->bte', d.astype(u_ext.dtype), pool_w[gi]))
    return jnp.concatenate(outs, axis=-1) * pool_scale

def rel_bucket(dist):
    max_exact = N_BUCKETS // 2
    d = jnp.maximum(dist, 1).astype(jnp.float32)
    large = max_exact + (jnp.log(d / max_exact) / math.log(MAX_DISTANCE / max_exact)
                         * (N_BUCKETS - max_exact)).astype(jnp.int32)
    return jnp.where(dist < max_exact, dist, jnp.minimum(large, N_BUCKETS - 1))

def indexer_select(qi, wi, ki, q_pos, k_pos, n_top):
    s = jnp.einsum('bqhd,bld->bqhl', qi.astype(jnp.float32), ki.astype(jnp.float32)) * IDX_DIM ** -0.5
    w = wi.astype(jnp.float32) * IDX_HEADS ** -0.5
    score = jnp.einsum('bqh,bqhl->bql', w, jax.nn.relu(s))
    score = jnp.where((k_pos[None, :] <= q_pos[:, None])[None], score, -jnp.inf)
    return lax.top_k(score, n_top)[1]

def attend(q, k_sel, v_sel, sel_pos, q_pos, rel_bias):
    B, Q = q.shape[:2]
    K = sel_pos.shape[-1]
    qg = q.reshape(B, Q, N_KV_HEADS, GROUP, HEAD_DIM)
    logits = jnp.einsum('bqcgd,bqkcd->bqcgk', qg, k_sel).astype(jnp.float32) * HEAD_DIM ** -0.5
    dist = q_pos[None, :, None] - sel_pos
    bias = rel_bias[rel_bucket(jnp.maximum(dist, 0))].astype(jnp.float32)
    bias = jnp.moveaxis(bias.reshape(B, Q, K, N_KV_HEADS, GROUP), 2, -1)
    valid = (dist >= 0)[:, :, None, None, :]
    probs = jax.nn.softmax(jnp.where(valid, logits + bias, -jnp.inf), axis=-1)
    out = jnp.einsum('bqcgk,bqkcd->bqcgd', probs.astype(v_sel.dtype), v_sel)
    return out.reshape(B, Q, ATTN_WIDTH)

def prompt_sparse_attention(q, k, v, qi, ki, wi, rel_bias):
    B, S = q.shape[:2]
    n_top = min(TOPK_MAX, S // 4)
    n_blk = S // Q_BLOCK
    k_pos = jnp.arange(S, dtype=jnp.int32)

    def to_blocks(a):
        return jnp.moveaxis(a.reshape((B, n_blk, Q_BLOCK) + a.shape[2:]), 1, 0)

    def one_block(args):
        qb, qib, wib, start = args
        q_pos = start + jnp.arange(Q_BLOCK, dtype=jnp.int32)
        idx = indexer_select(qib, wib, ki, q_pos, k_pos, n_top)
        k_sel = jax.vmap(lambda kb, ib: kb[ib])(k, idx)
        v_sel = jax.vmap(lambda vb, ib: vb[ib])(v, idx)
        return attend(qb, k_sel, v_sel, idx, q_pos, rel_bias)

    starts = jnp.arange(n_blk, dtype=jnp.int32) * Q_BLOCK
    out = lax.map(one_block, (to_blocks(q), to_blocks(qi), to_blocks(wi), starts))
    return jnp.moveaxis(out, 0, 1).reshape(B, S, ATTN_WIDTH)

def sample_sparse_attention(q, k_new, v_new, qi, ki_new, wi, cache_k, cache_v, cache_idx_k, page_table, rel_bias):
    B, T = q.shape[:2]
    n_past = page_table.shape[1] * PAGE_SIZE
    L = n_past + T
    n_top = min(TOPK_MAX, L // 4)
    ki_past = cache_idx_k[page_table].reshape(B, n_past, IDX_DIM)
    ki_all = jnp.concatenate([ki_past.astype(ki_new.dtype), ki_new], axis=1)
    q_pos = n_past + jnp.arange(T, dtype=jnp.int32)
    k_pos = jnp.arange(L, dtype=jnp.int32)
    idx = indexer_select(qi, wi, ki_all, q_pos, k_pos, n_top)
    in_past = (idx < n_past)[..., None, None]
    pidx = jnp.minimum(idx, n_past - 1)
    phys = jnp.take_along_axis(page_table, (pidx // PAGE_SIZE).reshape(B, -1), axis=1).reshape(pidx.shape)
    off = pidx % PAGE_SIZE
    nidx = jnp.clip(idx - n_past, 0, T - 1)
    k_sel = jnp.where(in_past, cache_k[phys, off].astype(k_new.dtype), jax.vmap(lambda kb, ib: kb[ib])(k_new, nidx))
    v_sel = jnp.where(in_past, cache_v[phys, off].astype(v_new.dtype), jax.vmap(lambda vb, ib: vb[ib])(v_new, nidx))
    return attend(q, k_sel, v_sel, idx, q_pos, rel_bias)

def merge_ffn(x, a_pool, a_attn, gates, w_pool_proj, w_attn_proj, w_out, ln2, w_gate_up, w_down):
    g = jax.nn.sigmoid(gates.astype(jnp.float32)).astype(x.dtype)
    m = (g[..., :D_MODEL] * jnp.einsum('bsc,cd->bsd', a_pool, w_pool_proj)
         + g[..., D_MODEL:] * jnp.einsum('bsc,cd->bsd', a_attn, w_attn_proj))
    h = x + jnp.einsum('bsd,de->bse', m, w_out)
    f = jnp.einsum('bsd,df->bsf', rms_norm(h, ln2), w_gate_up)
    return h + jnp.einsum('bsf,fd->bsd', jax.nn.silu(f[..., :D_FF]) * f[..., D_FF:], w_down)

def setup_inputs(seed: int = 0) -> dict:
    key = jax.random.key(seed)
    ks = jax.random.split(key, 20)
    n_pages = PAST_LEN // PAGE_SIZE
    n_phys = (DEC_BATCH * n_pages * 5) // 4

    def nrm(k, shape, scale):
        return jax.random.normal(k, shape, jnp.float32) * scale

    perm = jax.random.permutation(ks[0], n_phys)
    page_table = perm[:DEC_BATCH * n_pages].reshape(DEC_BATCH, n_pages).astype(jnp.int32)
    return {
        'x_prompt': nrm(ks[1], (BATCH, SEQ, D_MODEL), 1.0),
        'x_sample': nrm(ks[2], (DEC_BATCH, DEC_SEQ, D_MODEL), 1.0),
        'cache_k': nrm(ks[3], (DEPTH, n_phys, PAGE_SIZE, N_KV_HEADS, HEAD_DIM), 1.0),
        'cache_v': nrm(ks[4], (DEPTH, n_phys, PAGE_SIZE, N_KV_HEADS, HEAD_DIM), 1.0),
        'cache_idx_k': nrm(ks[5], (DEPTH, n_phys, PAGE_SIZE, IDX_DIM), 1.0),
        'state_pool': nrm(ks[6], (DEPTH, DEC_BATCH, POOL_BUF, POOL_WIDTH), 1.0),
        'page_table': page_table,
        'ln1': 1.0 + nrm(ks[7], (DEPTH, D_MODEL), 0.05),
        'w_in': nrm(ks[8], (DEPTH, D_MODEL, IN_WIDTH), D_MODEL ** -0.5),
        'pool_w': nrm(ks[9], (DEPTH, POOL_GROUPS, POOL_GROUP_DIM, POOL_GROUP_DIM), POOL_GROUP_DIM ** -0.5),
        'pool_scale': 1.0 + nrm(ks[10], (DEPTH, POOL_WIDTH), 0.1),
        'w_pool_proj': nrm(ks[11], (DEPTH, POOL_WIDTH, D_MODEL), POOL_WIDTH ** -0.5),
        'w_attn_proj': nrm(ks[12], (DEPTH, ATTN_WIDTH, D_MODEL), ATTN_WIDTH ** -0.5),
        'w_out': nrm(ks[13], (DEPTH, D_MODEL, D_MODEL), D_MODEL ** -0.5),
        'ln2': 1.0 + nrm(ks[14], (DEPTH, D_MODEL), 0.05),
        'w_gate_up': nrm(ks[15], (DEPTH, D_MODEL, 2 * D_FF), D_MODEL ** -0.5),
        'w_down': nrm(ks[16], (DEPTH, D_FF, D_MODEL), D_FF ** -0.5),
        'rel_bias': nrm(ks[17], (N_BUCKETS, N_HEADS), 0.5),
        'ln_final': 1.0 + nrm(ks[18], (D_MODEL,), 0.05),
    }

def reference(x_prompt, x_sample, cache_k, cache_v, cache_idx_k, state_pool, page_table, ln1, w_in, pool_w,
              pool_scale, w_pool_proj, w_attn_proj, w_out, ln2, w_gate_up, w_down, rel_bias, ln_final):
    n_past = page_table.shape[1] * PAGE_SIZE
    hp, hs = x_prompt, x_sample
    kp, vp, kip, pp, ksm, vsm, kism, psm = [], [], [], [], [], [], [], []
    for l in range(DEPTH):
        u, q, k, v, qi, ki, wi, gates = project_in(hp, ln1[l], w_in[l])
        a_pool = pool_mixer(u, 0, 0, pool_w[l], pool_scale[l])
        a_attn = prompt_sparse_attention(q, k, v, qi, ki, wi, rel_bias)
        kp.append(k); vp.append(v); kip.append(ki); pp.append(u[:, -POOL_BUF:])
        hp = merge_ffn(hp, a_pool, a_attn, gates, w_pool_proj[l], w_attn_proj[l], w_out[l], ln2[l], w_gate_up[l], w_down[l])
        u, q, k, v, qi, ki, wi, gates = project_in(hs, ln1[l], w_in[l])
        u_ext = jnp.concatenate([state_pool[l].astype(u.dtype), u], axis=1)
        a_pool = pool_mixer(u_ext, POOL_BUF, n_past, pool_w[l], pool_scale[l])
        a_attn = sample_sparse_attention(q, k, v, qi, ki, wi, cache_k[l], cache_v[l], cache_idx_k[l], page_table, rel_bias)
        ksm.append(k); vsm.append(v); kism.append(ki); psm.append(u_ext[:, -POOL_BUF:])
        hs = merge_ffn(hs, a_pool, a_attn, gates, w_pool_proj[l], w_attn_proj[l], w_out[l], ln2[l], w_gate_up[l], w_down[l])
    y_prompt = rms_norm(hp, ln_final)
    y_sample = rms_norm(hs, ln_final)
    new_k_prompt = jnp.stack(kp)
    new_v_prompt = jnp.stack(vp)
    new_idx_k_prompt = jnp.stack(kip)
    new_pool_prompt = jnp.stack(pp)
    new_k_sample = jnp.stack(ksm)
    new_v_sample = jnp.stack(vsm)
    new_idx_k_sample = jnp.stack(kism)
    new_pool_sample = jnp.stack(psm)
    return (y_prompt, y_sample, new_k_prompt, new_v_prompt, new_idx_k_prompt, new_pool_prompt,
            new_k_sample, new_v_sample, new_idx_k_sample, new_pool_sample)


_drawn_inputs = setup_inputs


def setup_inputs(seed=0):
    import zlib

    import numpy as np

    out = dict(_drawn_inputs(seed))
    spreads = {}
    factors = {}
    for name, (base, spread) in spreads.items():
        noise = np.random.default_rng([zlib.crc32(name.encode()), seed]).standard_normal(out[name].shape)
        drawn = base * np.exp(spread * noise) if base else spread * noise
        out[name] = __import__('jax').numpy.asarray(drawn.astype(out[name].dtype))
    for name, factor in factors.items():
        out[name] = (out[name] * factor).astype(out[name].dtype)
    return out
```

```python
import math
from contextlib import ExitStack

import concourse.bass as bass
from concourse import mybir

F32 = mybir.dt.float32
I32 = mybir.dt.int32
ALU = mybir.AluOpType
ACT = mybir.ActivationFunctionType
AX = mybir.AxisListType

P = 128
D = 1024
SEQ = 1024
NB = 8
TOK = SEQ + NB
KD = D // P
NCH = 3
CH = TOK // NCH
PW = 512
NG = 4
POOLBUF = 15
NH, NKV, HD = 8, 4, 64
IH = 4
TOPK = 256
PAGE = 128
NPAGES = 16
PAST = NPAGES * PAGE
SR = P // NPAGES
KR = PAST // P
DFF = 2816
NF = DFF // P
EPS = 1e-6
NBLK = SEQ // P
NT = NBLK + 1
C_U, C_Q, C_K, C_QI, C_G = 0, 512, 1024, 1536, 1860
NKVC = 2 * NKV * HD
NIDX = IH * HD + HD + IH
FIRST_TOPK = TOPK // P
NEG = -1.0e30
NONCAUSAL = -2.9e38
TAKEN = -3.0e38
NBUCKETS, MAXDIST = 32, 128
RW = 384


def bucket_starts():
    half = NBUCKETS // 2
    return list(range(half)) + [math.ceil(half * (MAXDIST / half) ** ((b - half) / half) - 1e-9)
                                for b in range(half, NBUCKETS)]


def rows(t):
    return P if t < NBLK else NB


def head_tile(h):
    g, r = divmod(h, 4)
    return 2 * g + r % 2, r // 2


def pieces(c):
    out, at = [], c * CH
    while at < (c + 1) * CH:
        t = at // P
        end = min((t + 1) * P, (c + 1) * CH)
        out.append((t, at - c * CH, at - t * P, end - t * P))
        at = end
    return out


def decoder_layer(nc, x_prompt, x_sample, cache_k, cache_v, cache_idx_k, state_pool, page_table, ln1, w_in,
                  pool_w, pool_scale, w_pool_proj, w_attn_proj, w_out, ln2, w_gate_up, w_down, rel_bias, ln_final,
                  y_prompt, y_sample, new_k_prompt, new_v_prompt, new_idx_k_prompt, new_pool_prompt,
                  new_k_sample, new_v_sample, new_idx_k_sample, new_pool_sample):
    xp, xs = x_prompt[0], x_sample.rearrange("b s d -> (b s) d")
    n_rows = cache_k.shape[1] * SR
    k_rows = cache_k.rearrange("l n (s r) h e -> (l n s) (r h e)", s=SR)
    v_rows = cache_v.rearrange("l n (s r) h e -> (l n s) (r h e)", s=SR)
    i_rows = cache_idx_k.rearrange("l n (s r) e -> (l n s) (r e)", s=SR)
    w_in_t = w_in[0].rearrange("(k p) n -> p k n", p=P)
    wpp_t = w_pool_proj[0].rearrange("(k p) n -> p k n", p=P)
    wap_t = w_attn_proj[0].rearrange("(g f e d) n -> f g d e n", g=2, f=2, e=2)
    wo_t = w_out[0].rearrange("(k p) n -> p k n", p=P)
    wgu_t = w_gate_up[0].rearrange("(k p) n -> p k n", p=P)
    wd_t = w_down[0].rearrange("(k p) n -> p k n", p=P)
    nk_p, nv_p = (a[0, 0].rearrange("s h e -> s (h e)") for a in (new_k_prompt, new_v_prompt))
    nk_s, nv_s = (a[0].rearrange("b s h e -> (b s) (h e)") for a in (new_k_sample, new_v_sample))
    ni_p, ni_s = new_idx_k_prompt[0, 0], new_idx_k_sample[0].rearrange("b s e -> (b s) e")
    bias_rows = nc.dram_tensor("bias_rows", [NH, P, RW], F32).ap()

    def tile_cols(t):
        return slice(t * P, t * P + rows(t))

    with ExitStack() as outer:
        def sb_in(ctx, name, shape, dt=F32):
            return ctx.enter_context(nc.sbuf_tensor(name, shape, dt))

        def sem_in(ctx, name):
            return ctx.enter_context(nc.semaphore(name))

        ps = outer.enter_context(nc.psum_tensor("banks", [P, 8, 512], F32))
        hT = sb_in(outer, "hT", [P, KD, TOK])
        ident = sb_in(outer, "ident", [P, P])
        ln2c = sb_in(outer, "ln2c", [P, KD])
        eps = sb_in(outer, "eps", [P, 1])

        def flat(b, n=2):
            return ps[:, b:b + n, :].rearrange("p a c -> p (a c)")

        with ExitStack() as ctx:
            def sb(name, shape, dt=F32):
                return sb_in(ctx, name, shape, dt)

            def sem(name):
                return sem_in(ctx, name)

            Z = sb("Z", [P, KD * TOK])
            w_kv = Z[:, 0:KD * NKVC].rearrange("p (k n) -> p k n", k=KD)
            w_ix = Z[:, KD * NKVC:KD * (NKVC + NIDX)].rearrange("p (k n) -> p k n", k=KD)
            k_ring = Z[:, 0:2 * KR * 256].rearrange("p (b n) -> p b n", b=2)
            M = Z[:, :].rearrange("p (k n) -> p k n", k=KD)
            UW = 16 + TOK
            UD = sb("UD", [P, NG * UW + NG * TOK])
            U = UD[:, 0:NG * UW].rearrange("p (g n) -> p g n", g=NG)
            Dp = UD[:, NG * UW:NG * UW + NG * TOK].rearrange("p (g n) -> p g n", g=NG)
            aP = UD[:, 0:NG * TOK].rearrange("p (g n) -> p g n", g=NG)
            T = UD[:, NG * UW:NG * UW + NH * 256].rearrange("p (h n) -> p h n", h=NH)
            v_ring = UD[:, 0:2 * KR * 256].rearrange("p (b n) -> p b n", b=2)
            xres = UD[:, 0:NBLK * D].rearrange("p (t n) -> p t n", t=NBLK)
            qT = sb("qT", [P, 4, TOK])
            kT = sb("kT", [P, 2, TOK])
            vN = sb("vN", [P, NT, 256])
            I = sb("I", [P, 3 * TOK])
            qiT = I[:, 0:2 * TOK].rearrange("p (k n) -> p k n", k=2)
            kiT = I[:, 2 * TOK:3 * TOK]
            S = I[0:64, 0:PAST + 1]
            lens = [(i + 1) * P for i in range(NBLK)]
            offs = [sum(lens[:i]) for i in range(NBLK)]
            SC = sb("SC", [P, sum(lens)])
            scs = [SC[:, offs[i]:offs[i] + lens[i]] for i in range(NBLK)]
            ss = sb("ss", [NB, PAST + 1])
            big = sb("big", [P, 2, KD, P])
            small = sb("small", [P, 2, 4, P])
            W = sb("W", [P, 4352])
            x_ring = W[:, 0:3 * D].rearrange("p (b n) -> p b n", b=3)
            kst = W[:, 3 * D:3 * D + 2 * 640].rearrange("p (b n) -> p b n", b=2)
            rl = W[:, 0:2048].rearrange("p (b n) -> p b n", b=2)
            kid = W[:, 0:2048].rearrange("p (b n) -> p b n", b=2)
            kidT = W[:, 2048:4096].rearrange("p (b n) -> p b n", b=2)
            KT = W[:, 0:2048].rearrange("p (b n) -> p b n", b=4)
            pool_tmp = W[:, 2048:2048 + 2 * 1040].rearrange("p (b n) -> p b n", b=2)
            gbuf = W[:, 0:2 * 3 * CH].rearrange("p (b c n) -> p b c n", b=2, c=3)
            pbuf = W[:, 2064:2064 + 2 * 3 * CH].rearrange("p (b c n) -> p b c n", b=2, c=3)
            lg = W[:, 0:2048].rearrange("p (b n) -> p b n", b=2)
            PTs = W[:, 2048:4096].rearrange("p (b n) -> p b n", b=2)
            PT = W[:, 0:KR * 64].rearrange("p (r n) -> p r n", r=KR)
            xs_res = SC[0:NB, 0:D]
            ZI = sb("ZI", [P, 576])
            ZQ = sb("ZQ", [P, 2, 576])
            onat = ZQ[:, 0, 0:512]
            ln1c = sb("ln1c", [P, KD])
            pscl = sb("pscl", [P, NG])
            poolw = I[:, 2576:2576 + NG * P].rearrange("p (g e) -> p g e", g=NG)
            wiN = sb("wiN", [P, NT, IH])
            stat = sb("stat", [P, 3, NT])
            top8 = sb("top8", [P, 8])
            qid = small[0:NB, 1, :, :].rearrange("p k n -> p (k n)").rearrange("p (h f d) -> p h f d", h=IH, f=2)
            zw = sb("zw", [NB, 64])
            wsel = sb("wsel", [64, NB])
            e8t = sb("e8t", [64, NB])
            e8 = sb("e8", [NB, 64])
            e8p = ZI[0:64, 0:NB]
            pd = ZI[0:NB, 64:128]
            rb = sb("rb", [64, NBUCKETS])
            R = sb("R", [64, RW])
            sx = small[:, 1, :, :].rearrange("p g (b t) -> p g b t", b=NB)
            st_nat = small[0:NB * POOLBUF, 0, :, :].rearrange("p k n -> p (k n)")
            sd = sb("sd", [P, NB])
            upo = I[0:POOLBUF + NB, 2052:2052 + PW]
            cfix = sb("cfix", [P, 16])
            pti = sb("pti", [P, NB], I32)
            sub_i = sb("sub_i", [P, 1], I32)
            sub_m = sb("sub_m", [P, 1], I32)
            sub_f = sb("sub_f", [P, 1])
            rowid = sb("rowid", [P, NB], I32)
            mx = sb("mx", [P, 2, 2])
            rs = sb("rs", [P, 2, NH])
            ri = sb("ri", [P, NH])
            smx = ZI[0:64, 128:132]
            rsn = sb("rsn", [32, 1])

            x_in = [sem(f"x_in{b}") for b in range(3)]
            consts_in = sem("consts_in"); nat_w_in = sem("nat_w_in")
            consts_made = sem("consts_made"); poolw_in = sem("poolw_in")
            x_squared = sem("x_squared"); x_root = sem("x_root"); x_scaled = sem("x_scaled"); rstd_ready = sem("rstd_ready")
            xT_ready = sem("xT_ready"); hT_ready = sem("hT_ready")
            nat_ready = sem("nat_ready"); nat_evac = sem("nat_evac"); natT_ready = sem("natT_ready"); natT_evac = sem("natT_evac")
            nat_out = [sem(f"nat_out{b}") for b in range(2)]
            idx_ready = sem("idx_ready"); relu_done = sem("relu_done"); score_step = sem("score_step"); causal_done = sem("causal_done")
            top_max = sem("top_max"); top_taken = sem("top_taken"); mask_ready = sem("mask_ready")
            rowid_ready = sem("rowid_ready")
            kid_in = [sem(f"kid_in{b}") for b in range(2)]
            kidT_ready = sem("kidT_ready"); kidT_evac = sem("kidT_evac"); kid_used = sem("kid_used")
            zi_step = sem("zi_step"); sidx_ready = sem("sidx_ready"); sidx_relu = sem("sidx_relu"); ssc_ready = sem("ssc_ready"); ss_ready = sem("ss_ready")
            big_in = [sem(f"big_in{b}") for b in range(2)]
            small_in = [sem(f"small_in{b}") for b in range(2)]
            uq_ready = sem("uq_ready"); uq_evac = sem("uq_evac")
            zq_ready = sem("zq_ready")
            k_in = [sem(f"k_in{b}") for b in range(2)]; k_used = sem("k_used")
            KT_ready = sem("KT_ready"); KT_evac = sem("KT_evac"); KT_used = sem("KT_used"); S_ready = sem("S_ready"); S_evac = sem("S_evac")
            st_in = sem("st_in"); stT_ready = sem("stT_ready"); stT_evac = sem("stT_evac")
            pool_out = sem("pool_out"); mix_step = sem("mix_step"); pooled = sem("pooled")
            uT_ready = sem("uT_ready"); uT_evac = sem("uT_evac"); ap_ready = sem("ap_ready"); ap_evac = sem("ap_evac")
            g_ready = sem("g_ready"); g_evac = sem("g_evac"); p_ready = sem("p_ready"); p_evac = sem("p_evac"); merged = sem("merged"); gated = sem("gated")
            bias_row = sem("bias_row"); bias_out = sem("bias_out"); T_in = sem("T_in")
            qk_ready = sem("qk_ready"); logit_done = sem("logit_done"); negmax = sem("negmax"); exp_done = sem("exp_done")
            pt_ready = sem("pt_ready"); pt_evac_a = sem("pt_evac_a"); pt_evac_v = sem("pt_evac_v"); pt_done = sem("pt_done"); pv_done = sem("pv_done")
            ri_ready = sem("ri_ready"); o_evac = sem("o_evac"); aT_ready = sem("aT_ready"); aT_evac = sem("aT_evac")
            sm_ready = sem("sm_ready"); sm_step = sem("sm_step"); sm_exp = sem("sm_exp"); sp_ready = sem("sp_ready"); sp_evac = sem("sp_evac")
            v_in = [sem(f"v_in{b}") for b in range(2)]; v_used = sem("v_used"); so_evac = sem("so_evac")
            xr_in = sem("xr_in"); wo_ready = sem("wo_ready"); wo_evac = sem("wo_evac")
            qid_ready = sem("qid_ready"); zi_ready = sem("zi_ready"); zi_copied = sem("zi_copied"); zw_made = sem("zw_made"); sidx_used = sem("sidx_used")
            pool_fill = sem("pool_fill"); row_fill = sem("row_fill"); row_calc = sem("row_calc")

            block = ctx.enter_context(nc.Block())
            U_ITEMS, Q_ITEMS = 4, 4
            NRND = TOPK // 8
            N_CONST_DMA = 3 + 2 * NB
            UNITS = NBLK * NH
            PTB = [-(-(i + 1) // 4) for i in range(NBLK)]

            def pt_base(n):
                i, h = divmod(n, NH)
                return NH * sum(PTB[:i]) + h * PTB[i]

            def wait_pt_evac(eng, count):
                eng.wait_ge(pt_evac_a, (count + 1) // 2)
                if count >= 2:
                    eng.wait_ge(pt_evac_v, count // 2)

            @block.sync
            def _(sp):
                for t in range(3):
                    sp.dma_start(x_ring[0:rows(t), t, :], xp[tile_cols(t), :]).then_inc(x_in[t], 16)
                sp.dma_start(w_kv, w_in_t[:, :, C_K:C_K + NKVC]).then_inc(nat_w_in, 16)
                sp.dma_start(w_ix, w_in_t[:, :, C_QI:C_QI + NIDX]).then_inc(nat_w_in, 16)
                for t in range(3, NT):
                    sp.wait_ge(xT_ready, 2 * (t - 3) + 2)
                    sp.dma_start(x_ring[0:rows(t), t % 3, :], xp[tile_cols(t), :] if t < NBLK else xs)\
                        .then_inc(x_in[t % 3], 16)
                sp.dma_start(st_nat, state_pool[0].rearrange("b t c -> (b t) c")).then_inc(st_in, 16)
                sp.dma_start(new_pool_sample[0, :, 0:POOLBUF - 1, :], state_pool[0, :, 1:POOLBUF, :]).then_inc(pool_out, 16)

                def slab_in(s, col):
                    sp.dma_start(big[:, s], w_in_t[:, :, col]).then_inc(big_in[s], 16)

                for n in range(U_ITEMS):
                    if n >= 2:
                        sp.wait_ge(uq_ready, 3 * (n - 1))
                    slab_in(n % 2, slice(C_U + n * P, C_U + (n + 1) * P))
                for j in range(Q_ITEMS):
                    n = U_ITEMS + j
                    sp.wait_ge(uq_ready, 3 * (n - 1))
                    for f in range(2):
                        h = 4 * (j // 2) + 2 * f + j % 2
                        sp.dma_start(big[:, n % 2, :, f * HD:(f + 1) * HD],
                                     w_in_t[:, :, C_Q + h * HD:C_Q + (h + 1) * HD]).then_inc(big_in[n % 2], 16)
                for s in range(2):
                    sp.wait_ge(uq_ready, 3 * (U_ITEMS + Q_ITEMS + s - 1))
                    slab_in(s, slice(C_G + s * P, C_G + (s + 1) * P))
                    if s == 1:
                        sp.wait_ge(pooled, NG)
                    sp.dma_start(small[:, s], wpp_t[:, :, s * P:(s + 1) * P]).then_inc(small_in[s], 16)
                with sp.Fori(1, KD // 2) as it:
                    for s in range(2):
                        gate_col, proj_col = sp.snap(it * (2 * P) + (C_G + s * P)), sp.snap(it * (2 * P) + s * P)
                        sp.wait_ge(p_ready, it * 6 + 3 * (s - 1))
                        slab_in(s, bass.ds(gate_col, P))
                        sp.dma_start(small[:, s], wpp_t[:, :, bass.ds(proj_col, P)]).then_inc(small_in[s], 16)
                with sp.Fori(0, KD // 2) as it:
                    for s in range(2):
                        gate_col, proj_col = sp.snap(it * (2 * P) + (C_G + D + s * P)), sp.snap(it * (2 * P) + s * P)
                        sp.wait_ge(p_ready, it * 6 + (24 + 3 * (s - 1)))
                        slab_in(s, bass.ds(gate_col, P))
                        for f in range(2):
                            for g in range(2):
                                for e in range(2):
                                    sp.dma_start(small[f * HD:(f + 1) * HD, s, 2 * g + e, :],
                                                 wap_t[f, g, :, e, bass.ds(proj_col, P)]).then_inc(small_in[s], 16)
                sp.wait_ge(v_used, NB)
                for t in range(NBLK):
                    sp.dma_start(xres[:, t, :], xp[tile_cols(t), :]).then_inc(xr_in, 16)
                sp.dma_start(xs_res, xs).then_inc(xr_in, 16)
                for m in range(KD):
                    if m < 2:
                        sp.wait_ge(g_ready, 24 + 3 * (KD - 1 + m))
                    else:
                        sp.wait_ge(wo_ready, 3 * (m - 1))
                    sp.dma_start(big[:, m % 2], wo_t[:, :, m * P:(m + 1) * P]).then_inc(big_in[m % 2], 16)
                sp.wait_ge(pool_out, 48)
                sp.wait_ge(bias_out, 16)
                for b in range(2):
                    sp.wait_ge(nat_out[b], 48 * len(range(b, NT, 2)))

            def wait_x(eng, t):
                eng.wait_ge(x_in[t % 3], 16 * (t // 3 + 1))

            @block.tensor
            def _(pe):
                mm, tr = nc.tensor.matmul, nc.tensor.transpose

                def transpose_x(t):
                    r = rows(t)
                    pe.wait_ge(x_scaled, t + 1)
                    if t:
                        pe.wait_ge(hT_ready, 2 * t)
                    for b in range(2):
                        for j in range(4):
                            k = 4 * b + j
                            last = tr(ps[:, b, j * P:j * P + r], x_ring[0:r, t % 3, k * P:(k + 1) * P], ident[0:r, 0:r])
                        last.then_inc(xT_ready, 1)

                def natural(t):
                    r = rows(t)
                    if t == 0:
                        pe.wait_ge(nat_w_in, 32)
                    pe.wait_ge(hT_ready, 2 * t + 2)
                    if t >= 2:
                        pe.wait_ge(nat_evac, t - 1)
                    for k in range(KD):
                        mm(ps[0:r, 4 + t % 2, 0:NKVC], hT[:, k, tile_cols(t)], w_kv[:, k, :], start=k == 0, stop=k == KD - 1)
                    for k in range(KD):
                        last = mm(ps[0:r, 6 + t % 2, 0:NIDX], hT[:, k, tile_cols(t)], w_ix[:, k, :], start=k == 0, stop=k == KD - 1)
                    last.then_inc(nat_ready, 1)

                def transpose_natural(t):
                    r = rows(t)
                    pe.wait_ge(nat_evac, t + 1)
                    if t:
                        pe.wait_ge(natT_evac, t)
                    for j in range(5):
                        last = tr(ps[:, 2 + j // 4, j % 4 * P:j % 4 * P + r], kst[0:r, t % 2, j * P:(j + 1) * P], ident[0:r, 0:r])
                    last.then_inc(natT_ready, 1)

                pe.wait_ge(consts_made, 1)
                transpose_x(0)
                for t in range(NT):
                    if t + 1 < NT:
                        transpose_x(t + 1)
                    natural(t)
                    if t >= 1:
                        transpose_natural(t - 1)
                transpose_natural(NT - 1)

                pe.wait_ge(natT_evac, NT)
                n = 0
                for i in range(FIRST_TOPK, NBLK):
                    for h in range(IH):
                        half = slice(h % 2 * HD, h % 2 * HD + HD)
                        if n >= 2:
                            pe.wait_ge(relu_done, n - 1)
                        for c0 in range(0, lens[i], 512):
                            w = min(512, lens[i] - c0)
                            last = mm(ps[:, 4 + 2 * (n % 2) + c0 // 512, 0:w], qiT[half, h // 2, tile_cols(i)],
                                      kiT[half, c0:c0 + w], start=True, stop=True)
                        last.then_inc(idx_ready, 1)
                        n += 1

                pe.wait_ge(qid_ready, 1)
                for h in range(IH):
                    last = tr(ps[:, 0, h * NB:(h + 1) * NB], qid[:, h, :, :].rearrange("p f d -> p (f d)"), ident[0:NB, 0:NB])
                last.then_inc(zi_ready, 1)
                pe.wait_ge(zw_made, 2)
                mm(ps[0:64, 1, 0:NB], zw[:, :], ident[0:NB, 0:NB], start=True, stop=True).then_inc(zi_ready, 1)
                pe.wait_ge(zi_copied, 1)
                pe.wait_ge(relu_done, n)
                for b in range(NB):
                    pe.wait_ge(kid_in[b % 2], 16 * (b // 2 + 1))
                    if b:
                        pe.wait_ge(kidT_evac, b)
                    for j in range(KR // 2):
                        last = tr(ps[:, j // 4, j % 4 * P:j % 4 * P + P], kid[:, b % 2, j * P:(j + 1) * P], ident[:, :])
                    last.then_inc(kid_used, 1)
                    pe.wait_ge(kidT_evac, b + 1)
                    for c in range(2):
                        mm(ps[0:64, 2 + c, :], ZI[:, 64 * b:64 * b + 64], kidT[:, b % 2, c * 512:(c + 1) * 512],
                           start=b == 0, stop=b == NB - 1)
                    last = mm(ps[0:32, 4, 0:1], ZI[0:HD, 64 * b:64 * b + 32], kiT[0:HD, SEQ + b:SEQ + b + 1],
                              start=b == 0, stop=b == NB - 1)
                    last.then_inc(sidx_used, 1)
                pe.wait_ge(sidx_relu, 1)
                for f in range(2):
                    for c in range(2):
                        mm(ps[0:NB, 4 + 2 * f + c, :], wsel[f * 32:(f + 1) * 32, :], kid[f * 32:(f + 1) * 32, 0, c * 512:(c + 1) * 512],
                           start=True, stop=True)
                mm(ps[0:NB, 0, 0:1], wsel[0:32, :], rsn[:, :], start=True, stop=True).then_inc(ssc_ready, 1)

                def slab_chunk(s, c, bank, done):
                    for k in range(KD):
                        last = mm(ps[:, bank, 0:CH], big[:, s, k, :], hT[:, k, c * CH:(c + 1) * CH], start=k == 0, stop=k == KD - 1)
                    last.then_inc(done, 1)
                    return last

                pe.wait_ge(ss_ready, 1)
                for first, per, at in ((0, 16, 0), (U_ITEMS, 32, 32)):
                    with pe.Fori(0, 2) as it:
                        for s in range(2):
                            pe.wait_ge(big_in[s], it * per + (at + per))
                            for c in range(NCH):
                                pe.wait_ge(uq_evac, it * 6 + (3 * first + 3 * s + c + 1))
                                slab_chunk(s, c, 3 * s + c, uq_ready)
                    if first == 0:
                        pe.wait_ge(st_in, 16)
                        for g in range(NG):
                            last = tr(ps[:, 6, g * 120:(g + 1) * 120], st_nat[:, g * P:(g + 1) * P], ident[0:120, 0:120])
                        last.then_inc(stT_ready, 1)
                        pe.wait_ge(uq_evac, 6 + 12)
                        for g in range(NG):
                            last = tr(ps[0:POOLBUF + NB, 7, g * P:(g + 1) * P], U[:, g, 16 + SEQ - POOLBUF:16 + TOK], ident[:, :])
                        last.then_inc(uT_ready, 1)

                pe.wait_ge(zq_ready, 1)
                pe.wait_ge(uq_evac, 6 + 24)
                pe.wait_ge(stT_evac, 1)
                pe.wait_ge(uT_evac, 1)
                chunks = [(b, rc, g) for b in range(NB) for rc in range(4) for g in range(2)]

                def key_logits(m):
                    b, rc, g = chunks[m]
                    pe.wait_ge(KT_evac, m + 1)
                    mm(ps[0:64, 4 + rc, :], ZQ[:, g, 64 * b:64 * b + 64], KT[:, m % 4, :],
                       start=(b == 0 and g == 0), stop=(b == NB - 1 and g == 1)).then_inc(KT_used, 1)

                for m, (b, rc, g) in enumerate(chunks):
                    if rc == 0 and g == 0:
                        pe.wait_ge(k_in[b % 2], 16 * (b // 2 + 1))
                    if m >= 2:
                        pe.wait_ge(KT_evac, m - 1)
                    for j in range(4):
                        at = (4 * rc + j) * 256 + g * P
                        last = tr(ps[:, m % 2, j * P:(j + 1) * P], k_ring[:, b % 2, at:at + P], ident[:, :])
                    last.then_inc(KT_ready, 1)
                    if m:
                        key_logits(m - 1)
                key_logits(len(chunks) - 1)
                for b in range(NB):
                    for g in range(2):
                        last = mm(ps[0:64, 2, 0:1], ZQ[:, g, 64 * b:64 * b + 64], kT[:, g, SEQ + b:SEQ + b + 1],
                                  start=(b == 0 and g == 0), stop=(b == NB - 1 and g == 1))
                last.then_inc(S_ready, 1)

                pe.wait_ge(poolw_in, 16)
                pe.wait_ge(S_evac, 1)
                pe.wait_ge(pooled, NG)
                for g in range(NG):
                    for c in range(NCH):
                        n = NCH * g + c
                        if n >= 4:
                            pe.wait_ge(ap_evac, n - 3)
                        mm(ps[:, n % 4, 0:CH], poolw[:, g, :], Dp[:, g, c * CH:(c + 1) * CH], start=True, stop=True).then_inc(ap_ready, 1)

                def merge_half(rhs, big_at, small_at, small_per, done):
                    with pe.Fori(0, KD // 2) as it:
                        for s in range(2):
                            pe.wait_ge(big_in[s], it * 16 + (big_at + 16))
                            for c in range(NCH):
                                pe.wait_ge(g_evac, it * 6 + (done + 3 * s + c + 1))
                                slab_chunk(s, c, c, g_ready)
                            pe.wait_ge(small_in[s], it * small_per + (small_at + small_per))
                            for c in range(NCH):
                                pe.wait_ge(p_evac, it * 6 + (done + 3 * s + c + 1))
                                for k in range(4):
                                    last = mm(ps[:, 3 + c, 0:CH], small[:, s, k, :], rhs[:, k, c * CH:(c + 1) * CH], start=k == 0, stop=k == 3)
                                last.then_inc(p_ready, 1)

                pe.wait_ge(ap_evac, NG * NCH)
                merge_half(aP, 96, 0, 16, 0)

                pe.wait_ge(g_evac, 3 + 24)
                pe.wait_ge(p_evac, 3 + 24)
                pe.wait_ge(T_in, 16)

                def logits(n):
                    i, h = divmod(n, NH)
                    t, f = head_tile(h)
                    half = slice(f * HD, (f + 1) * HD)
                    if n >= 2:
                        pe.wait_ge(logit_done, n - 1)
                    for c0 in range(0, lens[i], 512):
                        end = min(c0 + 512, lens[i])
                        bank = 2 * (n % 2) + c0 // 512
                        near = [c for c in (lens[i] - 2 * P, lens[i] - P) if c0 <= c < end]
                        last = mm(ps[:, bank, 0:end - c0], qT[half, t, tile_cols(i)], kT[half, h // 4, c0:end], start=True, stop=not near)
                        for c in near:
                            j = (c - (lens[i] - 2 * P))
                            last = mm(ps[:, bank, c - c0:c - c0 + P], ident[:, :], T[:, h, j:j + P], start=False, stop=c == near[-1])
                    last.then_inc(qk_ready, 1)

                def transpose_probs(n):
                    i = n // NH
                    pe.wait_ge(exp_done, n + 1)
                    for q in range(PTB[i]):
                        b = pt_base(n) + q
                        if b >= 2:
                            pe.wait_ge((pt_evac_a, pt_evac_v)[b % 2], b // 2)
                        for j in range(4 * q, min(4 * q + 4, i + 1)):
                            last = tr(ps[:, 4 + b % 2, j % 4 * P:j % 4 * P + P], lg[:, n % 2, j * P:(j + 1) * P], ident[:, :])
                        last.then_inc(pt_ready, 1)

                def times_values(n):
                    i, h = divmod(n, NH)
                    t, f = head_tile(h)
                    wait_pt_evac(pe, pt_base(n + 1) if n + 1 < UNITS else pt_base(n) + PTB[i])
                    if h == 0 and i:
                        pe.wait_ge(o_evac, i)
                    at = t * P + f * HD
                    for j in range(i + 1):
                        last = mm(ps[:, 6, at:at + HD], PTs[:, n % 2, j * P:(j + 1) * P], vN[:, j, (h // 2) * HD:(h // 2 + 1) * HD],
                                  start=j == 0, stop=j == i)
                    last.then_inc(pv_done, 1)

                def transpose_out(i):
                    pe.wait_ge(o_evac, i + 1)
                    if i:
                        pe.wait_ge(aT_evac, i)
                    for t in range(4):
                        last = tr(ps[:, 7, t * P:(t + 1) * P], onat[:, t * P:(t + 1) * P], ident[:, :])
                    last.then_inc(aT_ready, 1)

                logits(0)
                for n in range(UNITS):
                    if n + 1 < UNITS:
                        logits(n + 1)
                    transpose_probs(n)
                    if n:
                        times_values(n - 1)
                    if n >= NH and n % NH == 1:
                        transpose_out(n // NH - 1)
                times_values(UNITS - 1)
                transpose_out(NBLK - 1)

                pe.wait_ge(logit_done, UNITS)
                wait_pt_evac(pe, pt_base(UNITS - 1) + PTB[-1])
                pe.wait_ge(mask_ready, NBLK - FIRST_TOPK + 1)
                ss_r = ss[:, 0:PAST].rearrange("b (p r) -> b r p", r=KR)
                for rc in range(4):
                    mm(ps[0:64, rc, :], e8[:, :], ss_r[:, 4 * rc:4 * rc + 4, :], start=True, stop=True)
                mm(ps[0:64, 4, 0:1], e8[:, :], ss[:, PAST:PAST + 1], start=True, stop=True).then_inc(sm_ready, 1)
                pe.wait_ge(sm_step, 8)
                pe.wait_ge(aT_evac, NBLK)
                mm(ps[0:NB, 5, 0:64], e8p[:, :], ident[0:64, 0:64], start=True, stop=True)
                for r in range(KR):
                    last = tr(ps[:, 6 + r // 8, r % 8 * 64:r % 8 * 64 + 64], S[:, r * P:(r + 1) * P], ident[0:64, 0:64])
                last.then_inc(sp_ready, 1)
                pe.wait_ge(sp_evac, 1)
                for b in range(NB):
                    pe.wait_ge(v_in[b % 2], 16 * (b // 2 + 1))
                    for g in range(2):
                        out = ps[:, 0, (2 * b + g) * 4:(2 * b + g) * 4 + 4]
                        for r in range(KR):
                            at = r * 256 + g * P
                            mm(out, v_ring[:, b % 2, at:at + P], PT[:, r, 8 * b + 4 * g:8 * b + 4 * g + 4], start=r == 0, stop=False)
                        last = mm(out, vN[0:NB, NBLK, g * P:(g + 1) * P], pd[:, 8 * b + 4 * g:8 * b + 4 * g + 4], start=False, stop=True)
                    last.then_inc(v_used, 1)
                pe.wait_ge(so_evac, 1)
                merge_half(qT, 160, 64, 128, 24)

                pe.wait_ge(g_evac, 3 + 48)
                pe.wait_ge(p_evac, 3 + 48)
                pe.wait_ge(merged, 6 + 48)
                pe.wait_ge(xr_in, 16 * NT)
                for m in range(KD):
                    pe.wait_ge(big_in[m % 2], 224 + 16 * (m // 2 + 1))
                    for c in range(NCH):
                        n = NCH * m + c
                        if n >= 6:
                            pe.wait_ge(wo_evac, n - 5)
                        for k in range(KD):
                            mm(ps[:, n % 6, 0:CH], big[:, m % 2, k, :], M[:, k, c * CH:(c + 1) * CH], start=k == 0, stop=False)
                        todo = pieces(c)
                        for t, at, r0, r1 in todo:
                            src = xres[:, t, m * P:(m + 1) * P] if t < NBLK else xs_res[:, m * P:(m + 1) * P]
                            last = mm(ps[:, n % 6, at:at + r1 - r0], src, ident[0:rows(t), r0:r1], start=False, stop=t == todo[-1][0])
                        last.then_inc(wo_ready, 1)

            @block.gpsimd
            def _(pool):
                gp = nc.gpsimd
                gp.memset(ident[:, :], 0.0)
                gp.memset(ZI[:, :], 0.0)
                gp.memset(ZQ[:, :, :], 0.0)
                gp.memset(eps[:, :], EPS)
                gp.memset(e8[:, :], 1.0)
                gp.memset(e8t[:, :], 1.0)
                gp.memset(SC[:, 0:offs[FIRST_TOPK]], 0.0)
                gp.memset(U[:, :, 0:16], 0.0)
                gp.memset(R[:, :], 0.0)
                for t in range(15):
                    gp.memset(cfix[:, t:t + 1], 1.0 / (t + 1))
                gp.iota(sub_i[:, :], [[0, 1]], base=0, channel_multiplier=1).then_inc(pool_fill, 1)
                pool.wait_ge(pool_fill, 1)
                gp.affine_select(out=ident[:, :], in_=ident[:, :], compare_op=ALU.not_equal, fill=1.0, base=0,
                                 pattern=[[-1, P]], channel_multiplier=1).then_inc(consts_made, 1)
                gp.affine_select(out=e8[:, :], in_=e8[:, :], compare_op=ALU.is_ge, fill=0.0, base=0,
                                 pattern=[[1, 64]], channel_multiplier=-NH).then_inc(pool_fill, 1)
                gp.affine_select(out=e8t[:, :], in_=e8t[:, :], compare_op=ALU.is_ge, fill=0.0, base=0,
                                 pattern=[[-NH, NB]], channel_multiplier=1).then_inc(pool_fill, 1)
                pool.wait_ge(pool_fill, 3)
                gp.affine_select(out=e8[:, :], in_=e8[:, :], compare_op=ALU.is_ge, fill=0.0, base=NH - 1,
                                 pattern=[[-1, 64]], channel_multiplier=NH).then_inc(consts_made, 1)
                gp.affine_select(out=e8t[:, :], in_=e8t[:, :], compare_op=ALU.is_ge, fill=0.0, base=NH - 1,
                                 pattern=[[NH, NB]], channel_multiplier=-1).then_inc(consts_made, 1)
                for i in range(FIRST_TOPK):
                    d = scs[i][:, i * P:(i + 1) * P]
                    gp.affine_select(out=d, in_=d, compare_op=ALU.is_ge, fill=NEG, base=0, pattern=[[-1, P]],
                                     channel_multiplier=1).then_inc(consts_made, 1)
                pool.wait_ge(consts_in, 16 * N_CONST_DMA)
                starts = bucket_starts()
                for b in range(NBUCKETS):
                    end = starts[b + 1] if b + 1 < NBUCKETS else 256
                    gp.tensor_scalar(R[:, 256 - end:256 - starts[b]], rb[:, b:b + 1].to_broadcast([64, end - starts[b]]),
                                     rb[:, NBUCKETS - 1:NBUCKETS], None, ALU.subtract).then_inc(bias_row, 1)
                pool.wait_ge(bias_row, NBUCKETS)
                pool.dma_start(bias_rows, R[0:NH, :].unsqueeze(1).to_broadcast([NH, P, RW])).then_inc(bias_out, 16)

                pool.wait_ge(rowid_ready, 1)
                for b in range(NB):
                    if b < 2:
                        if b == 0:
                            pool.wait_ge(relu_done, IH * (NBLK - FIRST_TOPK))
                            pool.wait_ge(score_step, IH * (NBLK - FIRST_TOPK))
                    else:
                        pool.wait_ge(kid_used, b - 1)
                    gp.indirect_dma_start(kid[:, b % 2, :], None, i_rows, bass.IndirectOffsetOnAxis(rowid[:, b:b + 1], 0))\
                        .then_inc(kid_in[b % 2], 16)
                    if b == 0:
                        for i in range(FIRST_TOPK, NBLK):
                            pool.wait_ge(score_step, IH * (i - FIRST_TOPK + 1))
                            d = scs[i][:, i * P:(i + 1) * P]
                            gp.affine_select(out=d, in_=d, compare_op=ALU.is_ge, fill=NONCAUSAL, base=0, pattern=[[-1, P]],
                                             channel_multiplier=1).then_inc(causal_done, 1)
                        for f in range(2):
                            gp.tensor_tensor(zw[:, f * 32:(f + 1) * 32].rearrange("b (c h) -> b c h", c=NB),
                                             ident[0:NB, 0:NB].unsqueeze(2).to_broadcast([NB, NB, IH]),
                                             wiN[0:NB, NBLK, :].unsqueeze(1).to_broadcast([NB, NB, IH]), ALU.mult).then_inc(zw_made, 1)

                def load_k(b):
                    if b >= 2:
                        pool.wait_ge(KT_ready, 8 * (b - 1))
                    gp.indirect_dma_start(k_ring[:, b % 2, :], None, k_rows, bass.IndirectOffsetOnAxis(rowid[:, b:b + 1], 0))\
                        .then_inc(k_in[b % 2], 16)

                pool.wait_ge(nat_ready, NT)
                load_k(0)
                load_k(1)

                step = [0]

                def did(ins):
                    step[0] += 1
                    ins.then_inc(mix_step, 1)

                pool.wait_ge(uq_evac, 6 + 12)
                pool.wait_ge(stT_evac, 1)
                pool.wait_ge(sidx_used, NB)
                did(gp.tensor_copy(sx[:, :, :, POOLBUF], U[:, :, 16 + SEQ:16 + TOK]))
                for g in range(NG):
                    w = 2 << g
                    src, lag, b = U[:, g, :], 1, 0
                    while lag < w:
                        lo = 2 * lag - 1
                        if step[0] > 1:
                            pool.wait_ge(mix_step, step[0])
                        did(gp.tensor_tensor(pool_tmp[:, b, lo:16 + SEQ], src[:, lo:16 + SEQ], src[:, lo - lag:16 + SEQ - lag], ALU.add))
                        src, lag, b = pool_tmp[:, b, :], 2 * lag, 1 - b
                    sums = src[:, 16:16 + SEQ]
                    pool.wait_ge(mix_step, step[0])
                    did(gp.tensor_scalar(Dp[:, g, w - 1:SEQ], sums[:, w - 1:SEQ], 1.0 / w, None, ALU.mult))
                    did(gp.tensor_tensor(Dp[:, g, 0:w - 1], sums[:, 0:w - 1], cfix[:, 0:w - 1], ALU.mult))
                    part, lo = w // 2, 16 - w
                    while part:
                        pool.wait_ge(mix_step, step[0])
                        did(gp.tensor_tensor(sx[:, g, :, lo:lo + part], sx[:, g, :, lo:lo + part], sx[:, g, :, lo + part:lo + 2 * part], ALU.add))
                        part //= 2
                    pool.wait_ge(mix_step, step[0])
                    did(gp.tensor_scalar(sd[:, :], sx[:, g, :, lo], 1.0 / w, None, ALU.mult))
                    did(gp.tensor_tensor(Dp[:, g, 0:SEQ], Dp[:, g, 0:SEQ], U[:, g, 16:16 + SEQ], ALU.subtract))
                    pool.wait_ge(mix_step, step[0])
                    gp.tensor_tensor(Dp[:, g, SEQ:TOK], sd[:, :], U[:, g, 16 + SEQ:16 + TOK], ALU.subtract).then_inc(pooled, 1)
                    pool.wait_ge(pooled, g + 1)
                for b in range(2, NB):
                    load_k(b)

                pool.wait_ge(bias_out, 16)
                pool.wait_ge(ap_ready, NG * NCH)
                pool.dma_start(T, bass.AP(bias_rows.tensor, P - 1, [[RW - 1, P], [P * RW, NH], [1, 256]])).then_inc(T_in, 16)

                def load_v(b):
                    if b >= 2:
                        pool.wait_ge(v_used, b - 1)
                    gp.indirect_dma_start(v_ring[:, b % 2, :], None, v_rows, bass.IndirectOffsetOnAxis(rowid[:, b:b + 1], 0))\
                        .then_inc(v_in[b % 2], 16)

                pool.wait_ge(S_ready, 1)
                with pool.Fori(0, KD // 2) as it:
                    for s in range(2):
                        for c in range(NCH):
                            pool.wait_ge(p_evac, it * 6 + (3 + 3 * s + c + 1))
                            gp.tensor_tensor(M[:, bass.ds(it * 2 + s, 1), c * CH:(c + 1) * CH].rearrange("p a c -> p (a c)"),
                                             gbuf[:, s, c, :], pbuf[:, s, c, :], ALU.mult).then_inc(merged, 1)
                load_v(0)
                pool.wait_ge(qk_ready, UNITS)
                for b in range(1, NB):
                    load_v(b)
                with pool.Fori(0, KD // 2) as it:
                    for s in range(2):
                        for c in range(NCH):
                            pool.wait_ge(p_evac, it * 6 + (3 + 24 + 3 * s + c + 1))
                            m = M[:, bass.ds(it * 2 + s, 1), c * CH:(c + 1) * CH].rearrange("p a c -> p (a c)")
                            gp.tensor_tensor(m, m, pbuf[:, s, c, :], ALU.add).then_inc(merged, 1)

            @block.scalar
            def _(act):
                A = nc.scalar.activation
                with nc.allow_non_contiguous_dma(reason="small vectors laid out by partition"):
                    act.dma_start(ln1c[:, :], ln1[0].rearrange("(k p) -> p k", p=P)).then_inc(consts_in, 16)
                    act.dma_start(ln2c[:, :], ln2[0].rearrange("(k p) -> p k", p=P)).then_inc(consts_in, 16)
                    act.dma_start(pscl[:, :], pool_scale[0].rearrange("(k p) -> p k", p=P)).then_inc(consts_in, 16)
                    for b in range(NB):
                        act.dma_start(rb[b * NH:(b + 1) * NH, :], rel_bias.rearrange("n h -> h n")).then_inc(consts_in, 16)
                        act.dma_start(pti[:, b:b + 1], bass.AP(page_table.tensor, b * NPAGES, [[1, NPAGES], [0, SR], [1, 1]])).then_inc(consts_in, 16)

                def stats(t):
                    r = rows(t)
                    wait_x(act, t)
                    if t:
                        act.wait_ge(x_squared, t)
                    A(SC[0:r, D:2 * D], x_ring[0:r, t % 3, :], ACT.Square, accum_out=stat[0:r, 0, t:t + 1]).then_inc(x_squared, 1)
                    act.wait_ge(x_squared, t + 1)
                    A(stat[0:r, 1, t:t + 1], stat[0:r, 0, t:t + 1], ACT.Sqrt, bias=eps[0:r, :], scale=1.0 / D).then_inc(x_root, 1)

                def natural_out(t):
                    r, b = rows(t), t % 2
                    act.wait_ge(nat_ready, t + 1)
                    if t >= 2:
                        act.wait_ge(natT_ready, t - 1)
                        act.wait_ge(nat_out[b], 48 * (t // 2))
                    A(kst[0:r, b, 0:256], ps[0:r, 4 + b, 0:256], ACT.Copy)
                    A(vN[0:r, t, :], ps[0:r, 4 + b, 256:512], ACT.Copy)
                    A(kst[0:r, b, 256:512], ps[0:r, 6 + b, 0:256], ACT.Copy)
                    A(kst[0:r, b, 512:640].rearrange("p (f d) -> p f d", f=2),
                      ps[0:r, 6 + b, 256:320].unsqueeze(1).to_broadcast([r, 2, HD]), ACT.Copy)
                    A(wiN[0:r, t, :], ps[0:r, 6 + b, 320:324], ACT.Copy, scale=IH ** -0.5 * HD ** -0.5).then_inc(nat_evac, 1)
                    act.wait_ge(nat_evac, t + 1)
                    dst = [a[tile_cols(t), :] for a in (nk_p, nv_p, ni_p)] if t < NBLK else [nk_s, nv_s, ni_s]
                    act.dma_start(dst[0], kst[0:r, b, 0:256]).then_inc(nat_out[b], 16)
                    act.dma_start(dst[1], vN[0:r, t, :]).then_inc(nat_out[b], 16)
                    act.dma_start(dst[2], kst[0:r, b, 512:576]).then_inc(nat_out[b], 16)

                act.wait_ge(pool_fill, 1)
                stats(0)
                stats(1)
                for t in range(NT):
                    if t + 2 < NT:
                        stats(t + 2)
                    natural_out(t)

                n = 0
                for i in range(FIRST_TOPK, NBLK):
                    for h in range(IH):
                        act.wait_ge(idx_ready, n + 1)
                        if n >= 2:
                            act.wait_ge(score_step, n - 1)
                        A(rl[:, n % 2, 0:lens[i]], flat(4 + 2 * (n % 2))[:, 0:lens[i]], ACT.Relu).then_inc(relu_done, 1)
                        n += 1

                act.wait_ge(nat_evac, NT)
                A(qid, kst[0:NB, 0, 256:512].rearrange("p (h d) -> p h d", h=IH).unsqueeze(2).to_broadcast([NB, IH, 2, HD]),
                  ACT.Copy).then_inc(qid_ready, 1)
                act.wait_ge(zi_ready, 2)
                for f in range(2):
                    half = slice(f * HD, (f + 1) * HD)
                    A(ZI[half, 32 * f:32 * f + NB * (64 + IH)]
                      .rearrange("p (b c) -> p b c", b=NB)[:, :, 0:IH],
                      ps[half, 0, 0:32].rearrange("p (h b) -> p b h", h=IH), ACT.Copy)
                A(wsel[:, :], ps[0:64, 1, 0:NB], ACT.Copy).then_inc(zi_copied, 1)
                act.wait_ge(natT_ready, NT)
                for b in range(2):
                    act.wait_ge(nat_out[b], 48 * len(range(b, NT, 2)))
                for b in range(NB):
                    act.wait_ge(kid_used, b + 1)
                    if b >= 2:
                        act.wait_ge(sidx_used, b - 1)
                    A(kidT[:, b % 2, :], flat(0), ACT.Copy).then_inc(kidT_evac, 1)
                act.wait_ge(sidx_used, NB)
                act.dma_start(poolw, pool_w[0].rearrange("g c e -> c g e")).then_inc(poolw_in, 16)
                A(kid[0:64, 0, :], flat(2)[0:64], ACT.Relu)
                A(rsn[:, :], ps[0:32, 4, 0:1], ACT.Relu).then_inc(sidx_relu, 1)
                act.wait_ge(ssc_ready, 1)
                for f in range(2):
                    A(ss[:, 0:PAST].rearrange("b (p r f) -> b f r p", f=2, p=P)[:, f],
                      flat(4 + 2 * f)[0:NB].rearrange("b (r p) -> b r p", p=P), ACT.Copy)
                A(ss[:, PAST:PAST + 1], ps[0:NB, 0, 0:1], ACT.Copy).then_inc(ss_ready, 1)

                act.sem_inc(uq_evac, 6)
                act.sem_inc(g_evac, 3)
                act.sem_inc(p_evac, 3)
                act.sem_inc(merged, 6)

                with act.Fori(0, U_ITEMS // 2) as it:
                    for s in range(2):
                        for c in range(NCH):
                            act.wait_ge(uq_ready, it * 6 + (3 * s + c + 1))
                            A(U[:, bass.ds(it * 2 + s, 1), 16 + c * CH:16 + (c + 1) * CH].rearrange("p a c -> p (a c)"),
                              ps[:, 3 * s + c, 0:CH], ACT.Copy).then_inc(uq_evac, 1)
                act.wait_ge(stT_ready, 1)
                A(sx[:, :, :, 0:POOLBUF], ps[:, 6, 0:480].rearrange("p (g b t) -> p g b t", g=NG, b=NB), ACT.Copy).then_inc(stT_evac, 1)
                act.wait_ge(uT_ready, 1)
                A(upo[:, :], ps[0:POOLBUF + NB, 7, :], ACT.Copy).then_inc(uT_evac, 1)
                act.wait_ge(uT_evac, 1)
                act.dma_start(new_pool_prompt[0, 0], upo[0:POOLBUF, :]).then_inc(pool_out, 16)
                act.dma_start(new_pool_sample[0, :, POOLBUF - 1, :], upo[POOLBUF:POOLBUF + NB, :]).then_inc(pool_out, 16)
                with act.Fori(0, Q_ITEMS // 2) as it:
                    for s in range(2):
                        for c in range(NCH):
                            act.wait_ge(uq_ready, it * 6 + (12 + 3 * s + c + 1))
                            A(qT[:, bass.ds(it * 2 + s, 1), c * CH:(c + 1) * CH].rearrange("p a c -> p (a c)"),
                              ps[:, 3 * s + c, 0:CH], ACT.Copy, scale=HD ** -0.5).then_inc(uq_evac, 1)
                act.wait_ge(uq_evac, 6 + 24)
                for g in range(2):
                    for f in range(2):
                        half = slice(f * HD, (f + 1) * HD)
                        last = A(ZQ[half, g, :].rearrange("p (b c) -> p b c", b=NB)[:, :, 4 * g + 2 * f:4 * g + 2 * f + 2],
                                 qT[half, 2 * g:2 * g + 2, SEQ:TOK].rearrange("p e b -> p b e"), ACT.Copy)
                last.then_inc(zq_ready, 1)
                for m in range(8 * NB):
                    act.wait_ge(KT_ready, m + 1)
                    if m >= 4:
                        act.wait_ge(KT_used, m - 3)
                    A(KT[:, m % 4, :], ps[:, m % 2, :], ACT.Copy).then_inc(KT_evac, 1)
                act.wait_ge(S_ready, 1)
                A(S[:, 0:PAST], flat(4, 4)[0:64], ACT.Copy)
                A(S[:, PAST:PAST + 1], ps[0:64, 2, 0:1], ACT.Copy).then_inc(S_evac, 1)
                for n in range(NG * NCH):
                    g, c = divmod(n, NCH)
                    act.wait_ge(ap_ready, n + 1)
                    if n == 0:
                        act.wait_ge(pooled, NG)
                    A(aP[:, g, c * CH:(c + 1) * CH], ps[:, n % 4, 0:CH], ACT.Copy, scale=pscl[:, g:g + 1]).then_inc(ap_evac, 1)

                with act.Fori(0, KD // 2) as it:
                    for s in range(2):
                        for c in range(NCH):
                            act.wait_ge(g_ready, it * 6 + (3 * s + c + 1))
                            act.wait_ge(merged, it * 6 + (3 * s + c + 1))
                            A(gbuf[:, s, c, :], ps[:, c, 0:CH], ACT.Sigmoid).then_inc(g_evac, 1)
                        for c in range(NCH):
                            act.wait_ge(p_ready, it * 6 + (3 * s + c + 1))
                            A(pbuf[:, s, c, :], ps[:, 3 + c, 0:CH], ACT.Copy).then_inc(p_evac, 1)

                act.wait_ge(merged, 6 + 24)
                for n in range(UNITS):
                    i, h = divmod(n, NH)
                    t, f = head_tile(h)
                    act.wait_ge(negmax, n + 1)
                    if h == 0 and i >= 2:
                        act.wait_ge(ri_ready, i - 1)
                    A(lg[:, n % 2, 0:lens[i]], lg[:, n % 2, 0:lens[i]], ACT.Exp, bias=mx[:, n % 2, 1:2],
                      accum_out=rs[:, i % 2, 2 * t + f:2 * t + f + 1]).then_inc(exp_done, 1)
                    for q in range(PTB[i]):
                        b = pt_base(n) + q
                        if b % 2:
                            continue
                        act.wait_ge(pt_ready, b + 1)
                        if n >= 2:
                            act.wait_ge(pv_done, n - 1)
                        w = min(4, i + 1 - 4 * q) * P
                        A(PTs[:, n % 2, q * 512:q * 512 + w], ps[:, 4, 0:w], ACT.Copy).then_inc(pt_evac_a, 1)
                    if n >= NH and n % NH == 1:
                        blk = n // NH - 1
                        act.wait_ge(aT_ready, blk + 1)
                        A(qT[:, :, tile_cols(blk)], ps[:, 7, :].rearrange("p (t n) -> p t n", t=4), ACT.Copy).then_inc(aT_evac, 1)
                act.wait_ge(aT_ready, NBLK)
                A(qT[:, :, tile_cols(NBLK - 1)], ps[:, 7, :].rearrange("p (t n) -> p t n", t=4), ACT.Copy).then_inc(aT_evac, 1)

                act.wait_ge(sm_step, 5)
                A(S[:, :], S[:, :], ACT.Exp, bias=smx[:, 1:2], accum_out=smx[:, 2:3]).then_inc(sm_exp, 1)
                act.wait_ge(sp_ready, 1)
                A(pd[:, :], ps[0:NB, 5, 0:64], ACT.Copy)
                A(PT[:, :, :].rearrange("p r n -> p (r n)"), flat(6), ACT.Copy).then_inc(sp_evac, 1)
                act.wait_ge(v_used, NB)
                for f in range(2):
                    half = slice(f * HD, (f + 1) * HD)
                    for g in range(2):
                        last = A(qT[half, 2 * g:2 * g + 2, SEQ:TOK],
                                 ps[half, 0, 0:64].rearrange("p (b g f e) -> p g f e b", b=NB, g=2, f=2)[:, g, f], ACT.Copy)
                last.then_inc(so_evac, 1)

                with act.Fori(0, KD // 2) as it:
                    for s in range(2):
                        for c in range(NCH):
                            act.wait_ge(g_ready, it * 6 + (24 + 3 * s + c + 1))
                            act.wait_ge(p_evac, it * 6 + (24 + 3 * s + c + 1))
                            A(gbuf[:, s, c, :], ps[:, c, 0:CH], ACT.Sigmoid).then_inc(g_evac, 1)
                for n in range(KD * NCH):
                    m, c = divmod(n, NCH)
                    act.wait_ge(wo_ready, n + 1)
                    A(hT[:, m, c * CH:(c + 1) * CH], ps[:, n % 6, 0:CH], ACT.Copy).then_inc(wo_evac, 1)

            @block.vector
            def _(dve):
                V = nc.vector

                def scale_x(t):
                    r = rows(t)
                    dve.wait_ge(x_root, t + 1)
                    V.reciprocal(stat[0:r, 2, t:t + 1], stat[0:r, 1, t:t + 1]).then_inc(rstd_ready, 1)
                    dve.wait_ge(rstd_ready, t + 1)
                    V.tensor_scalar(x_ring[0:r, t % 3, :], x_ring[0:r, t % 3, :], stat[0:r, 2, t:t + 1], None, ALU.mult).then_inc(x_scaled, 1)

                def hT_out(t):
                    r = rows(t)
                    for b in range(2):
                        dve.wait_ge(xT_ready, 2 * t + b + 1)
                        V.tensor_tensor(hT[:, 4 * b:4 * b + 4, tile_cols(t)], ps[:, b, :].rearrange("p (k n) -> p k n", k=4)[:, :, 0:r],
                                        ln1c[:, 4 * b:4 * b + 4].unsqueeze(2).to_broadcast([P, 4, r]), ALU.mult).then_inc(hT_ready, 1)

                def naturalT_out(t):
                    r = rows(t)
                    dve.wait_ge(natT_ready, t + 1)
                    V.tensor_copy(kT[:, :, tile_cols(t)], ps[:, 2, 0:256].rearrange("p (k n) -> p k n", k=2)[:, :, 0:r])
                    V.tensor_copy(qiT[:, :, tile_cols(t)], ps[:, 2, 256:512].rearrange("p (k n) -> p k n", k=2)[:, :, 0:r])
                    V.tensor_copy(kiT[:, tile_cols(t)], ps[:, 3, 0:r]).then_inc(natT_evac, 1)

                dve.wait_ge(consts_in, 16 * N_CONST_DMA)
                dve.wait_ge(pool_fill, 1)
                V.tensor_scalar(sub_m[:, :], sub_i[:, :], SR - 1, None, ALU.bitwise_and).then_inc(row_calc, 1)
                dve.wait_ge(row_calc, 1)
                V.tensor_copy(sub_f[:, :], sub_m[:, :]).then_inc(row_calc, 1)
                dve.wait_ge(row_calc, 2)
                V.tensor_scalar(rowid[:, :], pti[:, :], float(SR), sub_f[:, :], ALU.mult, ALU.add).then_inc(rowid_ready, 1)

                scale_x(0)
                scale_x(1)
                hT_out(0)
                for t in range(NT):
                    if t + 2 < NT:
                        scale_x(t + 2)
                    if t + 1 < NT:
                        hT_out(t + 1)
                    if t >= 1:
                        naturalT_out(t - 1)
                naturalT_out(NT - 1)

                dve.wait_ge(nat_evac, NT)
                n = 0
                for i in range(FIRST_TOPK, NBLK):
                    for h in range(IH):
                        dve.wait_ge(relu_done, n + 1)
                        src, w = rl[:, n % 2, 0:lens[i]], wiN[:, i, h:h + 1]
                        if h == 0:
                            V.tensor_scalar(scs[i], src, w, None, ALU.mult).then_inc(score_step, 1)
                        else:
                            dve.wait_ge(score_step, n)
                            V.scalar_tensor_tensor(scs[i], src, w, scs[i], ALU.mult, ALU.add).then_inc(score_step, 1)
                        n += 1

                def select(k, sc, r):
                    for n in range(k * NRND, (k + 1) * NRND):
                        if n:
                            dve.wait_ge(top_taken, n)
                        V.max(top8[0:r, :], sc).then_inc(top_max, 1)
                        dve.wait_ge(top_max, n + 1)
                        V.match_replace(sc, top8[0:r, :], sc, TAKEN).then_inc(top_taken, 1)
                    dve.wait_ge(top_taken, (k + 1) * NRND)
                    V.tensor_scalar(sc, sc, TAKEN, NEG, ALU.not_equal, ALU.mult).then_inc(mask_ready, 1)

                for k, i in enumerate(range(FIRST_TOPK, NBLK)):
                    dve.wait_ge(causal_done, k + 1)
                    select(k, scs[i], P)
                dve.wait_ge(ss_ready, 1)
                select(NBLK - FIRST_TOPK, ss[:, :], NB)

                def row_max(n):
                    i = n // NH
                    dve.wait_ge(qk_ready, n + 1)
                    if n >= 2:
                        dve.wait_ge(pt_ready, pt_base(n - 1))
                    if n == 0:
                        dve.wait_ge(merged, 6 + 24)
                    V.tensor_tensor_reduce(lg[:, n % 2, 0:lens[i]], flat(2 * (n % 2))[:, 0:lens[i]], scs[i], 1.0, 3 * NEG,
                                           ALU.add, ALU.max, mx[:, n % 2, 0:1]).then_inc(logit_done, 1)
                    dve.wait_ge(logit_done, n + 1)
                    V.tensor_scalar(mx[:, n % 2, 1:2], mx[:, n % 2, 0:1], -1.0, None, ALU.mult).then_inc(negmax, 1)

                def out_block(i):
                    dve.wait_ge(pv_done, NH * (i + 1))
                    dve.wait_ge(exp_done, NH * (i + 1))
                    V.reciprocal(ri[:, :], rs[:, i % 2, :]).then_inc(ri_ready, 1)
                    dve.wait_ge(ri_ready, i + 1)
                    if i:
                        dve.wait_ge(aT_ready, i)
                    V.tensor_tensor(onat[:, :].rearrange("p (h d) -> p h d", h=NH), ps[:, 6, :].rearrange("p (h d) -> p h d", h=NH),
                                    ri[:, :].unsqueeze(2).to_broadcast([P, NH, HD]), ALU.mult).then_inc(o_evac, 1)

                row_max(0)
                for n in range(UNITS):
                    i = n // NH
                    if n + 1 < UNITS:
                        row_max(n + 1)
                    for q in range(PTB[i]):
                        b = pt_base(n) + q
                        if b % 2 == 0:
                            continue
                        dve.wait_ge(pt_ready, b + 1)
                        if n >= 2:
                            dve.wait_ge(pv_done, n - 1)
                        w = min(4, i + 1 - 4 * q) * P
                        V.tensor_copy(PTs[:, n % 2, q * 512:q * 512 + w], ps[:, 5, 0:w]).then_inc(pt_evac_v, 1)
                    if n >= NH and n % NH == 0:
                        out_block(n // NH - 1)
                out_block(NBLK - 1)

                dve.wait_ge(sm_ready, 1)
                dve.wait_ge(S_evac, 1)
                V.tensor_tensor(S[:, 0:PAST], S[:, 0:PAST], flat(0, 4)[0:64], ALU.add).then_inc(sm_step, 1)
                dve.wait_ge(bias_row, NBUCKETS)
                V.scalar_tensor_tensor(S[:, PAST:PAST + 1], S[:, PAST:PAST + 1], R[:, 255:256], ps[0:64, 4, 0:1],
                                       ALU.add, ALU.add).then_inc(sm_step, 1)
                dve.wait_ge(sm_step, 2)
                near = S[:, 0:PAST].rearrange("k (r p) -> k r p", p=P)[:, :, P - P // KR:P]
                V.tensor_tensor(near, near, R[:, P - 1:P - 1 + P].rearrange("k (p r) -> k r p", r=KR), ALU.add).then_inc(sm_step, 1)
                dve.wait_ge(sm_step, 3)
                V.tensor_reduce(smx[:, 0:1], S[:, :], AX.X, ALU.max).then_inc(sm_step, 1)
                dve.wait_ge(sm_step, 4)
                V.tensor_scalar(smx[:, 1:2], smx[:, 0:1], -1.0, None, ALU.mult).then_inc(sm_step, 1)
                dve.wait_ge(sm_exp, 1)
                V.reciprocal(smx[:, 3:4], smx[:, 2:3]).then_inc(sm_step, 1)
                dve.wait_ge(sm_step, 6)
                V.tensor_scalar(S[:, :], S[:, :], smx[:, 3:4], None, ALU.mult).then_inc(sm_step, 1)
                dve.wait_ge(sm_step, 7)
                dve.wait_ge(consts_made, 3)
                V.tensor_scalar(e8p[:, :], e8t[:, :], S[:, PAST:PAST + 1], None, ALU.mult).then_inc(sm_step, 1)

                with dve.Fori(0, KD // 2) as it:
                    for s in range(2):
                        for c in range(NCH):
                            dve.wait_ge(p_ready, it * 6 + (24 + 3 * s + c + 1))
                            dve.wait_ge(g_evac, it * 6 + (3 + 24 + 3 * s + c + 1))
                            dve.wait_ge(merged, it * 6 + (24 + 3 * s + c + 1))
                            V.tensor_tensor(pbuf[:, s, c, :], ps[:, 3 + c, 0:CH], gbuf[:, s, c, :], ALU.mult).then_inc(p_evac, 1)

        with ExitStack() as ctx:
            def sb(name, shape, dt=F32):
                return sb_in(ctx, name, shape, dt)

            def sem(name):
                return sem_in(ctx, name)

            hn = sb("hn", [P, KD, TOK])
            act_t = sb("act_t", [P, NF, TOK])
            WS = sb("WS", [P, 2 * NF * P])
            gu = WS[:, 0:4 * KD * P].rearrange("p (s a k n) -> p s a k n", s=2, a=2, k=KD)
            down = WS[:, :].rearrange("p (s k n) -> p s k n", s=2, k=NF)
            TMP = sb("TMP", [P, 4 * D])
            sq = TMP[:, 0:4 * CH].rearrange("p (b n) -> p b n", b=4)
            root = TMP[:, 4 * CH:7 * CH].rearrange("p (c n) -> p c n", c=NCH)
            rinv = TMP[:, 7 * CH:10 * CH].rearrange("p (c n) -> p c n", c=NCH)
            sg = TMP[:, 0:6 * CH].rearrange("p (s c n) -> p s c n", s=2, c=NCH)
            yo = TMP[:, 0:2 * D].rearrange("p (b n) -> p b n", b=2)
            junk = TMP[:, 2 * D:3 * D]
            lnf = TMP[:, 3 * D:4 * D]
            ones = sb("ones", [P, P])
            fst = sb("fst", [P, 3, NT])

            ones_made = sem("ones_made"); sq_done = sem("sq_done"); ssq_ready = sem("ssq_ready"); sq_used = sem("sq_used")
            root_done = sem("root_done"); rinv_done = sem("rinv_done"); hn_ready = sem("hn_ready")
            gu_in = [sem(f"gu_in{b}") for b in range(2)]
            gate_ready = sem("gate_ready"); up_ready = sem("up_ready"); silu_done = sem("silu_done"); act_done = sem("act_done")
            down_in = [sem(f"down_in{b}") for b in range(2)]; down_ready = sem("down_ready"); y_done = sem("y_done")
            lnf_in = sem("lnf_in"); yT_ready = sem("yT_ready"); fsq = sem("fsq"); froot = sem("froot"); frinv = sem("frinv"); y_ready = sem("y_ready")
            y_out = [sem(f"y_out{b}") for b in range(2)]

            block = ctx.enter_context(nc.Block())

            @block.sync
            def _(sp):
                for s in range(2):
                    for a in range(2):
                        sp.dma_start(gu[:, s, a], wgu_t[:, :, a * DFF + s * P:a * DFF + (s + 1) * P]).then_inc(gu_in[s], 16)
                with sp.Fori(1, NF // 2) as it:
                    for s in range(2):
                        cols = [sp.snap(it * (2 * P) + (a * DFF + s * P)) for a in range(2)]
                        sp.wait_ge(up_ready, it * 6 + 3 * (s - 1))
                        for a in range(2):
                            sp.dma_start(gu[:, s, a], wgu_t[:, :, bass.ds(cols[a], P)]).then_inc(gu_in[s], 16)
                sp.wait_ge(up_ready, NCH * NF)
                for s in range(2):
                    sp.dma_start(down[:, s], wd_t[:, :, s * P:(s + 1) * P]).then_inc(down_in[s], 16)
                sp.wait_ge(act_done, NCH * NF)
                sp.dma_start(lnf, bass.AP(ln_final.tensor, 0, [[0, P], [1, D]])).then_inc(lnf_in, 16)
                with sp.Fori(1, KD // 2) as it:
                    for s in range(2):
                        col = sp.snap(it * (2 * P) + s * P)
                        sp.wait_ge(down_ready, it * 6 + 3 * (s - 1))
                        sp.dma_start(down[:, s], wd_t[:, :, bass.ds(col, P)]).then_inc(down_in[s], 16)
                for t in range(NT):
                    sp.wait_ge(y_ready, t + 1)
                    dst = y_prompt[0, tile_cols(t), :] if t < NBLK else y_sample.rearrange("b s d -> (b s) d")
                    sp.dma_start(dst, yo[0:rows(t), t % 2, :]).then_inc(y_out[t % 2], 16)
                for b in range(2):
                    sp.wait_ge(y_out[b], 16 * len(range(b, NT, 2)))

            @block.tensor
            def _(pe):
                mm, tr = nc.tensor.matmul, nc.tensor.transpose
                pe.wait_ge(ones_made, 1)
                for n in range(NCH * KD):
                    c, k = divmod(n, KD)
                    pe.wait_ge(sq_done, n + 1)
                    last = mm(ps[:, c, 0:CH], ones[:, :], sq[:, n % 4, :], start=k == 0, stop=k == KD - 1).then_inc(sq_used, 1)
                pe.wait_ge(root_done, NCH)
                with pe.Fori(0, NF // 2) as it:
                    for s in range(2):
                        pe.wait_ge(gu_in[s], it * 32 + 32)
                        for c in range(NCH):
                            pe.wait_ge(hn_ready, KD * (c + 1))
                            for a, done, out in ((0, silu_done, gate_ready), (1, act_done, up_ready)):
                                pe.wait_ge(done, it * 6 + (3 * s + c + 1))
                                for k in range(KD):
                                    last = mm(ps[:, 3 * a + c, 0:CH], gu[:, s, a, k, :], hn[:, k, c * CH:(c + 1) * CH], start=k == 0, stop=k == KD - 1)
                                last.then_inc(out, 1)
                pe.wait_ge(act_done, 3 + NCH * NF)
                with pe.Fori(0, KD // 2) as it:
                    for s in range(2):
                        pe.wait_ge(down_in[s], it * 16 + 16)
                        for c in range(NCH):
                            pe.wait_ge(y_done, it * 6 + (3 * s + c + 1))
                            for k in range(NF):
                                last = mm(ps[:, 3 * s + c, 0:CH], down[:, s, k, :], act_t[:, k, c * CH:(c + 1) * CH], start=k == 0, stop=k == NF - 1)
                            last.then_inc(down_ready, 1)
                pe.wait_ge(y_done, 6 + NCH * KD)
                for t in range(NT):
                    r = rows(t)
                    if t >= 4:
                        pe.wait_ge(y_ready, t - 3)
                    for k in range(KD):
                        last = tr(ps[0:r, 2 * (t % 4) + k // 4, k % 4 * P:k % 4 * P + P], hT[:, k, tile_cols(t)], ident[:, :])
                    last.then_inc(yT_ready, 1)

            @block.gpsimd
            def _(pool):
                nc.gpsimd.memset(ones[:, :], 1.0).then_inc(ones_made, 1)

            @block.scalar
            def _(act):
                A = nc.scalar.activation
                for n in range(NCH * KD):
                    c, k = divmod(n, KD)
                    if n >= 4:
                        act.wait_ge(sq_used, n - 3)
                    A(sq[:, n % 4, :], hT[:, k, c * CH:(c + 1) * CH], ACT.Square).then_inc(sq_done, 1)
                for c in range(NCH):
                    act.wait_ge(sq_used, KD * (c + 1))
                    A(root[:, c, :], ps[:, c, 0:CH], ACT.Sqrt, bias=eps[:, :], scale=1.0 / D).then_inc(root_done, 1)
                act.sem_inc(silu_done, 3)
                act.wait_ge(hn_ready, NCH * KD)
                with act.Fori(0, NF // 2) as it:
                    for s in range(2):
                        for c in range(NCH):
                            act.wait_ge(gate_ready, it * 6 + (3 * s + c + 1))
                            act.wait_ge(act_done, it * 6 + (3 * s + c + 1))
                            A(sg[:, s, c, :], ps[:, c, 0:CH], ACT.Silu).then_inc(silu_done, 1)
                act.wait_ge(act_done, 3 + NCH * NF)
                for t in range(NT):
                    r = rows(t)
                    act.wait_ge(yT_ready, t + 1)
                    if t:
                        act.wait_ge(fsq, t)
                    A(junk[0:r, :], flat(2 * (t % 4))[0:r], ACT.Square, accum_out=fst[0:r, 0, t:t + 1]).then_inc(fsq, 1)
                    act.wait_ge(fsq, t + 1)
                    A(fst[0:r, 1, t:t + 1], fst[0:r, 0, t:t + 1], ACT.Sqrt, bias=eps[0:r, :], scale=1.0 / D).then_inc(froot, 1)

            @block.vector
            def _(dve):
                V = nc.vector
                dve.sem_inc(act_done, 3)
                dve.sem_inc(y_done, 6)
                for c in range(NCH):
                    dve.wait_ge(root_done, c + 1)
                    V.reciprocal(rinv[:, c, :], root[:, c, :]).then_inc(rinv_done, 1)
                    dve.wait_ge(rinv_done, c + 1)
                    for k in range(KD):
                        V.scalar_tensor_tensor(hn[:, k, c * CH:(c + 1) * CH], hT[:, k, c * CH:(c + 1) * CH], ln2c[:, k:k + 1], rinv[:, c, :],
                                               ALU.mult, ALU.mult).then_inc(hn_ready, 1)
                with dve.Fori(0, NF // 2) as it:
                    for s in range(2):
                        for c in range(NCH):
                            dve.wait_ge(silu_done, it * 6 + (3 + 3 * s + c + 1))
                            dve.wait_ge(up_ready, it * 6 + (3 * s + c + 1))
                            V.tensor_tensor(act_t[:, bass.ds(it * 2 + s, 1), c * CH:(c + 1) * CH].rearrange("p a c -> p (a c)"),
                                            ps[:, 3 + c, 0:CH], sg[:, s, c, :], ALU.mult).then_inc(act_done, 1)
                with dve.Fori(0, KD // 2) as it:
                    for s in range(2):
                        for c in range(NCH):
                            dve.wait_ge(down_ready, it * 6 + (3 * s + c + 1))
                            m = hT[:, bass.ds(it * 2 + s, 1), c * CH:(c + 1) * CH].rearrange("p a c -> p (a c)")
                            V.tensor_tensor(m, m, ps[:, 3 * s + c, 0:CH], ALU.add).then_inc(y_done, 1)
                dve.wait_ge(lnf_in, 16)
                for t in range(NT):
                    r = rows(t)
                    dve.wait_ge(froot, t + 1)
                    V.reciprocal(fst[0:r, 2, t:t + 1], fst[0:r, 1, t:t + 1]).then_inc(frinv, 1)
                    dve.wait_ge(frinv, t + 1)
                    if t >= 2:
                        dve.wait_ge(y_out[t % 2], 16 * (t // 2))
                    V.scalar_tensor_tensor(yo[0:r, t % 2, :], flat(2 * (t % 4))[0:r], fst[0:r, 2, t:t + 1], lnf[0:r, :],
                                           ALU.mult, ALU.mult).then_inc(y_ready, 1)


_INS = ["x_prompt", "x_sample", "cache_k", "cache_v", "cache_idx_k", "state_pool", "page_table", "ln1", "w_in", "pool_w",
        "pool_scale", "w_pool_proj", "w_attn_proj", "w_out", "ln2", "w_gate_up", "w_down", "rel_bias", "ln_final"]
_OUTS = [(1, SEQ, D), (NB, 1, D), (1, 1, SEQ, NKV, HD), (1, 1, SEQ, NKV, HD), (1, 1, SEQ, HD), (1, 1, POOLBUF, PW),
         (1, NB, 1, NKV, HD), (1, NB, 1, NKV, HD), (1, NB, 1, HD), (1, NB, POOLBUF, PW)]


def kernel(**inputs):
    import numpy as _np
    import concourse.bacc as _bacc
    from concourse.bass_utils import run_bass_kernel_spmd as _run

    nc = _bacc.Bacc("TRN2", target_bir_lowering=False, num_devices=1)
    arrays, args = {}, []
    for name in _INS:
        a = _np.ascontiguousarray(inputs[name])
        arrays[f"in_{name}_dram"] = a
        args.append(nc.dram_tensor(f"in_{name}_dram", a.shape, mybir.dt.from_np(a.dtype), kind="ExternalInput").ap())
    for i, shape in enumerate(_OUTS):
        args.append(nc.dram_tensor(f"out_{i}_dram", shape, F32, kind="ExternalOutput").ap())
    decoder_layer(nc, *args)
    r = _run(nc, [arrays], core_ids=[0])
    return tuple(r.results[0][f"out_{i}_dram"] for i in range(len(_OUTS)))
```

```python
import math
from contextlib import ExitStack

import concourse.bass as bass
from concourse import mybir

F32 = mybir.dt.float32
F32R = mybir.dt.float32r
I32 = mybir.dt.int32
ALU = mybir.AluOpType
ACT = mybir.ActivationFunctionType
AX = mybir.AxisListType

P = 128
D = 1024
SEQ = 1024
NB = 8
TOK = SEQ + NB
KD = D // P
NCH = 3
CH = TOK // NCH
PW = 512
NG = 4
POOLBUF = 15
NH, NKV, HD = 8, 4, 64
IH = 4
TOPK = 256
PAGE = 128
NPAGES = 16
PAST = NPAGES * PAGE
SR = P // NPAGES
KR = PAST // P
DFF = 2816
NF = DFF // P
EPS = 1e-6
NBLK = SEQ // P
NT = NBLK + 1
C_U, C_Q, C_K, C_QI, C_G = 0, 512, 1024, 1536, 1860
NKVC = 2 * NKV * HD
NIDX = IH * HD + HD + IH
FIRST_TOPK = TOPK // P
NEG = -1.0e30
NONCAUSAL = -2.9e38
TAKEN = -3.0e38
NBUCKETS, MAXDIST = 32, 128
RW = 384


def bucket_starts():
    half = NBUCKETS // 2
    return list(range(half)) + [math.ceil(half * (MAXDIST / half) ** ((b - half) / half) - 1e-9)
                                for b in range(half, NBUCKETS)]


def rows(t):
    return P if t < NBLK else NB


def head_tile(h):
    g, r = divmod(h, 4)
    return 2 * g + r % 2, r // 2


def pieces(c):
    out, at = [], c * CH
    while at < (c + 1) * CH:
        t = at // P
        end = min((t + 1) * P, (c + 1) * CH)
        out.append((t, at - c * CH, at - t * P, end - t * P))
        at = end
    return out


def decoder_layer(nc, x_prompt, x_sample, cache_k, cache_v, cache_idx_k, state_pool, page_table, ln1, w_in,
                  pool_w, pool_scale, w_pool_proj, w_attn_proj, w_out, ln2, w_gate_up, w_down, rel_bias, ln_final,
                  y_prompt, y_sample, new_k_prompt, new_v_prompt, new_idx_k_prompt, new_pool_prompt,
                  new_k_sample, new_v_sample, new_idx_k_sample, new_pool_sample):
    xp, xs = x_prompt[0], x_sample.rearrange("b s d -> (b s) d")
    n_rows = cache_k.shape[1] * SR
    k_rows = cache_k.rearrange("l n (s r) h e -> (l n s) (r h e)", s=SR)
    v_rows = cache_v.rearrange("l n (s r) h e -> (l n s) (r h e)", s=SR)
    i_rows = cache_idx_k.rearrange("l n (s r) e -> (l n s) (r e)", s=SR)
    w_in_t = w_in[0].rearrange("(k p) n -> p k n", p=P)
    wpp_t = w_pool_proj[0].rearrange("(k p) n -> p k n", p=P)
    wap_t = w_attn_proj[0].rearrange("(g f e d) n -> f g d e n", g=2, f=2, e=2)
    wo_t = w_out[0].rearrange("(k p) n -> p k n", p=P)
    wgu_t = w_gate_up[0].rearrange("(k p) n -> p k n", p=P)
    wd_t = w_down[0].rearrange("(k p) n -> p k n", p=P)
    nk_p, nv_p = (a[0, 0].rearrange("s h e -> s (h e)") for a in (new_k_prompt, new_v_prompt))
    nk_s, nv_s = (a[0].rearrange("b s h e -> (b s) (h e)") for a in (new_k_sample, new_v_sample))
    ni_p, ni_s = new_idx_k_prompt[0, 0], new_idx_k_sample[0].rearrange("b s e -> (b s) e")
    bias_rows = nc.dram_tensor("bias_rows", [NH, P, RW], F32).ap()

    def tile_cols(t):
        return slice(t * P, t * P + rows(t))

    def product(out, w_cols, x_cols, nk):
        for k in range(nk):
            for j, (w, x) in enumerate((("hi", "hi"), ("hi", "lo"), ("lo", "hi"))):
                last = nc.tensor.matmul(out, w_cols(w, k), x_cols(x, k), start=(k == 0 and j == 0), stop=(k == nk - 1 and j == 2))
        return last

    with ExitStack() as outer:
        def sb_in(ctx, name, shape, dt=F32):
            return ctx.enter_context(nc.sbuf_tensor(name, shape, dt))

        def sem_in(ctx, name):
            return ctx.enter_context(nc.semaphore(name))

        ps = outer.enter_context(nc.psum_tensor("banks", [P, 8, 512], F32))
        hT = sb_in(outer, "hT", [P, KD, TOK])
        ident = sb_in(outer, "ident", [P, P])
        ln2c = sb_in(outer, "ln2c", [P, KD])
        eps = sb_in(outer, "eps", [P, 1])

        def flat(b, n=2):
            return ps[:, b:b + n, :].rearrange("p a c -> p (a c)")

        def chunk(c):
            return slice(c * CH, (c + 1) * CH)

        def f32(ap):
            return ap.bitcast(F32)

        middle = ExitStack()
        Z = sb_in(middle, "Z", [P, KD * TOK])
        M = Z[:, :].rearrange("p (k n) -> p k n", k=KD)
        qT = sb_in(middle, "qT", [P, 4, TOK])

        with ExitStack() as ctx:
            def sb(name, shape, dt=F32):
                return sb_in(ctx, name, shape, dt)

            def sem(name):
                return sem_in(ctx, name)

            w_kv = Z[:, 0:KD * NKVC].rearrange("p (k n) -> p k n", k=KD)
            w_ix = Z[:, KD * NKVC:KD * (NKVC + NIDX)].rearrange("p (k n) -> p k n", k=KD)
            k_ring = Z[:, 0:2 * KR * 256].rearrange("p (b n) -> p b n", b=2)
            UW = 16 + TOK
            UD = sb("UD", [P, NG * UW + NG * TOK])
            U = UD[:, 0:NG * UW].rearrange("p (g n) -> p g n", g=NG)
            Dp = UD[:, NG * UW:NG * UW + NG * TOK].rearrange("p (g n) -> p g n", g=NG)
            aP = UD[:, 0:NG * TOK].rearrange("p (g n) -> p g n", g=NG)
            T = UD[:, NG * UW:NG * UW + NH * 256].rearrange("p (h n) -> p h n", h=NH)
            v_ring = UD[:, 0:2 * KR * 256].rearrange("p (b n) -> p b n", b=2)
            kT = sb("kT", [P, 2, TOK])
            vN = sb("vN", [P, NT, 256])
            I = sb("I", [P, 3 * TOK])
            qiT = I[:, 0:2 * TOK].rearrange("p (k n) -> p k n", k=2)
            kiT = I[:, 2 * TOK:3 * TOK]
            S = I[0:64, 0:PAST + 1]
            lens = [(i + 1) * P for i in range(NBLK)]
            offs = [sum(lens[:i]) for i in range(NBLK)]
            SC = sb("SC", [P, sum(lens)])
            scs = [SC[:, offs[i]:offs[i] + lens[i]] for i in range(NBLK)]
            ss = sb("ss", [NB, PAST + 1])
            big = sb("big", [P, 2, KD, P])
            small = sb("small", [P, 2, 4, P])
            W = sb("W", [P, 4352])
            x_ring = W[:, 0:3 * D].rearrange("p (b n) -> p b n", b=3)
            kst = W[:, 3 * D:3 * D + 2 * 640].rearrange("p (b n) -> p b n", b=2)
            rl = W[:, 0:2048].rearrange("p (b n) -> p b n", b=2)
            kid = W[:, 0:2048].rearrange("p (b n) -> p b n", b=2)
            kidT = W[:, 2048:4096].rearrange("p (b n) -> p b n", b=2)
            KT = W[:, 0:2048].rearrange("p (b n) -> p b n", b=4)
            pool_tmp = W[:, 2048:2048 + 2 * 1040].rearrange("p (b n) -> p b n", b=2)
            gbuf = W[:, 0:2 * 3 * CH].rearrange("p (b c n) -> p b c n", b=2, c=3)
            pbuf = W[:, 2064:2064 + 2 * 3 * CH].rearrange("p (b c n) -> p b c n", b=2, c=3)
            lg = W[:, 0:2048].rearrange("p (b n) -> p b n", b=2)
            PTs = W[:, 2048:4096].rearrange("p (b n) -> p b n", b=2)
            PT = W[:, 0:KR * 64].rearrange("p (r n) -> p r n", r=KR)
            ZI = sb("ZI", [P, 576])
            ZQ = sb("ZQ", [P, 2, 576])
            onat = ZQ[:, 0, 0:512]
            ln1c = sb("ln1c", [P, KD])
            pscl = sb("pscl", [P, NG])
            poolw = I[:, 2576:2576 + NG * P].rearrange("p (g e) -> p g e", g=NG)
            wiN = sb("wiN", [P, NT, IH])
            stat = sb("stat", [P, 3, NT])
            top8 = sb("top8", [P, 8])
            qid = small[0:NB, 1, :, :].rearrange("p k n -> p (k n)").rearrange("p (h f d) -> p h f d", h=IH, f=2)
            zw = sb("zw", [NB, 64])
            wsel = sb("wsel", [64, NB])
            e8t = sb("e8t", [64, NB])
            e8 = sb("e8", [NB, 64])
            e8p = ZI[0:64, 0:NB]
            pd = ZI[0:NB, 64:128]
            rb = sb("rb", [64, NBUCKETS])
            R = sb("R", [64, RW])
            sx = small[:, 1, :, :].rearrange("p g (b t) -> p g b t", b=NB)
            st_nat = small[0:NB * POOLBUF, 0, :, :].rearrange("p k n -> p (k n)")
            sd = sb("sd", [P, NB])
            upo = I[0:POOLBUF + NB, 2052:2052 + PW]
            cfix = sb("cfix", [P, 16])
            pti = sb("pti", [P, NB], I32)
            sub_i = sb("sub_i", [P, 1], I32)
            sub_m = sb("sub_m", [P, 1], I32)
            sub_f = sb("sub_f", [P, 1])
            rowid = sb("rowid", [P, NB], I32)
            mx = sb("mx", [P, 2, 2])
            rs = sb("rs", [P, 2, NH])
            ri = sb("ri", [P, NH])
            smx = ZI[0:64, 128:132]
            rsn = sb("rsn", [32, 1])

            x_in = [sem(f"x_in{b}") for b in range(3)]
            consts_in = sem("consts_in"); nat_w_in = sem("nat_w_in")
            consts_made = sem("consts_made"); poolw_in = sem("poolw_in")
            x_squared = sem("x_squared"); x_root = sem("x_root"); x_scaled = sem("x_scaled"); rstd_ready = sem("rstd_ready")
            xT_ready = sem("xT_ready"); hT_ready = sem("hT_ready")
            nat_ready = sem("nat_ready"); nat_evac = sem("nat_evac"); natT_ready = sem("natT_ready"); natT_evac = sem("natT_evac")
            nat_out = [sem(f"nat_out{b}") for b in range(2)]
            idx_ready = sem("idx_ready"); relu_done = sem("relu_done"); score_step = sem("score_step"); causal_done = sem("causal_done")
            top_max = sem("top_max"); top_taken = sem("top_taken"); mask_ready = sem("mask_ready")
            rowid_ready = sem("rowid_ready")
            kid_in = [sem(f"kid_in{b}") for b in range(2)]
            kidT_ready = sem("kidT_ready"); kidT_evac = sem("kidT_evac"); kid_used = sem("kid_used")
            zi_step = sem("zi_step"); sidx_ready = sem("sidx_ready"); sidx_relu = sem("sidx_relu"); ssc_ready = sem("ssc_ready"); ss_ready = sem("ss_ready")
            big_in = [sem(f"big_in{b}") for b in range(2)]
            small_in = [sem(f"small_in{b}") for b in range(2)]
            uq_ready = sem("uq_ready"); uq_evac = sem("uq_evac")
            zq_ready = sem("zq_ready")
            k_in = [sem(f"k_in{b}") for b in range(2)]; k_used = sem("k_used")
            KT_ready = sem("KT_ready"); KT_evac = sem("KT_evac"); KT_used = sem("KT_used"); S_ready = sem("S_ready"); S_evac = sem("S_evac")
            st_in = sem("st_in"); stT_ready = sem("stT_ready"); stT_evac = sem("stT_evac")
            pool_out = sem("pool_out"); mix_step = sem("mix_step"); pooled = sem("pooled")
            uT_ready = sem("uT_ready"); uT_evac = sem("uT_evac"); ap_ready = sem("ap_ready"); ap_evac = sem("ap_evac")
            g_ready = sem("g_ready"); g_evac = sem("g_evac"); p_ready = sem("p_ready"); p_evac = sem("p_evac"); merged = sem("merged")
            bias_row = sem("bias_row"); bias_out = sem("bias_out"); T_in = sem("T_in")
            qk_ready = sem("qk_ready"); logit_done = sem("logit_done"); negmax = sem("negmax"); exp_done = sem("exp_done")
            pt_ready = sem("pt_ready"); pt_evac_a = sem("pt_evac_a"); pt_evac_v = sem("pt_evac_v"); pt_done = sem("pt_done"); pv_done = sem("pv_done")
            ri_ready = sem("ri_ready"); o_evac = sem("o_evac"); aT_ready = sem("aT_ready"); aT_evac = sem("aT_evac")
            sm_ready = sem("sm_ready"); sm_step = sem("sm_step"); sm_exp = sem("sm_exp"); sp_ready = sem("sp_ready"); sp_evac = sem("sp_evac")
            v_in = [sem(f"v_in{b}") for b in range(2)]; v_used = sem("v_used"); so_evac = sem("so_evac")
            qid_ready = sem("qid_ready"); zi_ready = sem("zi_ready"); zi_copied = sem("zi_copied"); zw_made = sem("zw_made"); sidx_used = sem("sidx_used")
            pool_fill = sem("pool_fill"); row_fill = sem("row_fill"); row_calc = sem("row_calc")

            block = ctx.enter_context(nc.Block())
            U_ITEMS, Q_ITEMS = 4, 4
            NRND = TOPK // 8
            N_CONST_DMA = 3 + 2 * NB
            UNITS = NBLK * NH
            PTB = [-(-(i + 1) // 4) for i in range(NBLK)]

            def pt_base(n):
                i, h = divmod(n, NH)
                return NH * sum(PTB[:i]) + h * PTB[i]

            def wait_pt_evac(eng, count):
                eng.wait_ge(pt_evac_a, (count + 1) // 2)
                if count >= 2:
                    eng.wait_ge(pt_evac_v, count // 2)

            @block.sync
            def _(sp):
                for t in range(3):
                    sp.dma_start(x_ring[0:rows(t), t, :], xp[tile_cols(t), :]).then_inc(x_in[t], 16)
                sp.dma_start(w_kv, w_in_t[:, :, C_K:C_K + NKVC]).then_inc(nat_w_in, 16)
                sp.dma_start(w_ix, w_in_t[:, :, C_QI:C_QI + NIDX]).then_inc(nat_w_in, 16)
                for t in range(3, NT):
                    sp.wait_ge(xT_ready, 2 * (t - 3) + 2)
                    sp.dma_start(x_ring[0:rows(t), t % 3, :], xp[tile_cols(t), :] if t < NBLK else xs)\
                        .then_inc(x_in[t % 3], 16)
                sp.dma_start(st_nat, state_pool[0].rearrange("b t c -> (b t) c")).then_inc(st_in, 16)
                sp.dma_start(new_pool_sample[0, :, 0:POOLBUF - 1, :], state_pool[0, :, 1:POOLBUF, :]).then_inc(pool_out, 16)

                def slab_in(s, col):
                    sp.dma_start(big[:, s], w_in_t[:, :, col]).then_inc(big_in[s], 16)

                for n in range(U_ITEMS):
                    if n >= 2:
                        sp.wait_ge(uq_ready, 3 * (n - 1))
                    slab_in(n % 2, slice(C_U + n * P, C_U + (n + 1) * P))
                for j in range(Q_ITEMS):
                    n = U_ITEMS + j
                    sp.wait_ge(uq_ready, 3 * (n - 1))
                    for f in range(2):
                        h = 4 * (j // 2) + 2 * f + j % 2
                        sp.dma_start(big[:, n % 2, :, f * HD:(f + 1) * HD],
                                     w_in_t[:, :, C_Q + h * HD:C_Q + (h + 1) * HD]).then_inc(big_in[n % 2], 16)
                for s in range(2):
                    sp.wait_ge(uq_ready, 3 * (U_ITEMS + Q_ITEMS + s - 1))
                    slab_in(s, slice(C_G + s * P, C_G + (s + 1) * P))
                    if s == 1:
                        sp.wait_ge(pooled, NG)
                    sp.dma_start(small[:, s], wpp_t[:, :, s * P:(s + 1) * P]).then_inc(small_in[s], 16)
                with sp.Fori(1, KD // 2) as it:
                    for s in range(2):
                        gate_col, proj_col = sp.snap(it * (2 * P) + (C_G + s * P)), sp.snap(it * (2 * P) + s * P)
                        sp.wait_ge(p_ready, it * 6 + 3 * (s - 1))
                        slab_in(s, bass.ds(gate_col, P))
                        sp.dma_start(small[:, s], wpp_t[:, :, bass.ds(proj_col, P)]).then_inc(small_in[s], 16)
                sp.wait_ge(pool_out, 48)
                sp.wait_ge(bias_out, 16)
                for b in range(2):
                    sp.wait_ge(nat_out[b], 48 * len(range(b, NT, 2)))

            def wait_x(eng, t):
                eng.wait_ge(x_in[t % 3], 16 * (t // 3 + 1))

            @block.tensor
            def _(pe):
                mm, tr = nc.tensor.matmul, nc.tensor.transpose

                def transpose_x(t):
                    r = rows(t)
                    pe.wait_ge(x_scaled, t + 1)
                    if t:
                        pe.wait_ge(hT_ready, 2 * t)
                    for b in range(2):
                        for j in range(4):
                            k = 4 * b + j
                            last = tr(ps[:, b, j * P:j * P + r], x_ring[0:r, t % 3, k * P:(k + 1) * P], ident[0:r, 0:r])
                        last.then_inc(xT_ready, 1)

                def natural(t):
                    r = rows(t)
                    if t == 0:
                        pe.wait_ge(nat_w_in, 32)
                    pe.wait_ge(hT_ready, 2 * t + 2)
                    if t >= 2:
                        pe.wait_ge(nat_evac, t - 1)
                    for k in range(KD):
                        mm(ps[0:r, 4 + t % 2, 0:NKVC], hT[:, k, tile_cols(t)], w_kv[:, k, :], start=k == 0, stop=k == KD - 1)
                    for k in range(KD):
                        last = mm(ps[0:r, 6 + t % 2, 0:NIDX], hT[:, k, tile_cols(t)], w_ix[:, k, :], start=k == 0, stop=k == KD - 1)
                    last.then_inc(nat_ready, 1)

                def transpose_natural(t):
                    r = rows(t)
                    pe.wait_ge(nat_evac, t + 1)
                    if t:
                        pe.wait_ge(natT_evac, t)
                    for j in range(5):
                        last = tr(ps[:, 2 + j // 4, j % 4 * P:j % 4 * P + r], kst[0:r, t % 2, j * P:(j + 1) * P], ident[0:r, 0:r])
                    last.then_inc(natT_ready, 1)

                pe.wait_ge(consts_made, 1)
                transpose_x(0)
                for t in range(NT):
                    if t + 1 < NT:
                        transpose_x(t + 1)
                    natural(t)
                    if t >= 1:
                        transpose_natural(t - 1)
                transpose_natural(NT - 1)

                pe.wait_ge(natT_evac, NT)
                n = 0
                for i in range(FIRST_TOPK, NBLK):
                    for h in range(IH):
                        half = slice(h % 2 * HD, h % 2 * HD + HD)
                        if n >= 2:
                            pe.wait_ge(relu_done, n - 1)
                        for c0 in range(0, lens[i], 512):
                            w = min(512, lens[i] - c0)
                            last = mm(ps[:, 4 + 2 * (n % 2) + c0 // 512, 0:w], qiT[half, h // 2, tile_cols(i)],
                                      kiT[half, c0:c0 + w], start=True, stop=True)
                        last.then_inc(idx_ready, 1)
                        n += 1

                pe.wait_ge(qid_ready, 1)
                for h in range(IH):
                    last = tr(ps[:, 0, h * NB:(h + 1) * NB], qid[:, h, :, :].rearrange("p f d -> p (f d)"), ident[0:NB, 0:NB])
                last.then_inc(zi_ready, 1)
                pe.wait_ge(zw_made, 2)
                mm(ps[0:64, 1, 0:NB], zw[:, :], ident[0:NB, 0:NB], start=True, stop=True).then_inc(zi_ready, 1)
                pe.wait_ge(zi_copied, 1)
                pe.wait_ge(relu_done, n)
                for b in range(NB):
                    pe.wait_ge(kid_in[b % 2], 16 * (b // 2 + 1))
                    if b:
                        pe.wait_ge(kidT_evac, b)
                    for j in range(KR // 2):
                        last = tr(ps[:, j // 4, j % 4 * P:j % 4 * P + P], kid[:, b % 2, j * P:(j + 1) * P], ident[:, :])
                    last.then_inc(kid_used, 1)
                    pe.wait_ge(kidT_evac, b + 1)
                    for c in range(2):
                        mm(ps[0:64, 2 + c, :], ZI[:, 64 * b:64 * b + 64], kidT[:, b % 2, c * 512:(c + 1) * 512],
                           start=b == 0, stop=b == NB - 1)
                    last = mm(ps[0:32, 4, 0:1], ZI[0:HD, 64 * b:64 * b + 32], kiT[0:HD, SEQ + b:SEQ + b + 1],
                              start=b == 0, stop=b == NB - 1)
                    last.then_inc(sidx_used, 1)
                pe.wait_ge(sidx_relu, 1)
                for f in range(2):
                    for c in range(2):
                        mm(ps[0:NB, 4 + 2 * f + c, :], wsel[f * 32:(f + 1) * 32, :], kid[f * 32:(f + 1) * 32, 0, c * 512:(c + 1) * 512],
                           start=True, stop=True)
                mm(ps[0:NB, 0, 0:1], wsel[0:32, :], rsn[:, :], start=True, stop=True).then_inc(ssc_ready, 1)

                def slab_chunk(s, c, bank, done):
                    for k in range(KD):
                        last = mm(ps[:, bank, 0:CH], big[:, s, k, :], hT[:, k, c * CH:(c + 1) * CH], start=k == 0, stop=k == KD - 1)
                    last.then_inc(done, 1)
                    return last

                pe.wait_ge(ss_ready, 1)
                for first, per, at in ((0, 16, 0), (U_ITEMS, 32, 32)):
                    with pe.Fori(0, 2) as it:
                        for s in range(2):
                            pe.wait_ge(big_in[s], it * per + (at + per))
                            for c in range(NCH):
                                pe.wait_ge(uq_evac, it * 6 + (3 * first + 3 * s + c + 1))
                                slab_chunk(s, c, 3 * s + c, uq_ready)
                    if first == 0:
                        pe.wait_ge(st_in, 16)
                        for g in range(NG):
                            last = tr(ps[:, 6, g * 120:(g + 1) * 120], st_nat[:, g * P:(g + 1) * P], ident[0:120, 0:120])
                        last.then_inc(stT_ready, 1)
                        pe.wait_ge(uq_evac, 6 + 12)
                        for g in range(NG):
                            last = tr(ps[0:POOLBUF + NB, 7, g * P:(g + 1) * P], U[:, g, 16 + SEQ - POOLBUF:16 + TOK], ident[:, :])
                        last.then_inc(uT_ready, 1)

                pe.wait_ge(zq_ready, 1)
                pe.wait_ge(uq_evac, 6 + 24)
                pe.wait_ge(stT_evac, 1)
                pe.wait_ge(uT_evac, 1)
                chunks = [(b, rc, g) for b in range(NB) for rc in range(4) for g in range(2)]

                def key_logits(m):
                    b, rc, g = chunks[m]
                    pe.wait_ge(KT_evac, m + 1)
                    mm(ps[0:64, 4 + rc, :], ZQ[:, g, 64 * b:64 * b + 64], KT[:, m % 4, :],
                       start=(b == 0 and g == 0), stop=(b == NB - 1 and g == 1)).then_inc(KT_used, 1)

                for m, (b, rc, g) in enumerate(chunks):
                    if rc == 0 and g == 0:
                        pe.wait_ge(k_in[b % 2], 16 * (b // 2 + 1))
                    if m >= 2:
                        pe.wait_ge(KT_evac, m - 1)
                    for j in range(4):
                        at = (4 * rc + j) * 256 + g * P
                        last = tr(ps[:, m % 2, j * P:(j + 1) * P], k_ring[:, b % 2, at:at + P], ident[:, :])
                    last.then_inc(KT_ready, 1)
                    if m:
                        key_logits(m - 1)
                key_logits(len(chunks) - 1)
                for b in range(NB):
                    for g in range(2):
                        last = mm(ps[0:64, 2, 0:1], ZQ[:, g, 64 * b:64 * b + 64], kT[:, g, SEQ + b:SEQ + b + 1],
                                  start=(b == 0 and g == 0), stop=(b == NB - 1 and g == 1))
                last.then_inc(S_ready, 1)

                pe.wait_ge(poolw_in, 16)
                pe.wait_ge(S_evac, 1)
                pe.wait_ge(pooled, NG)
                for g in range(NG):
                    for c in range(NCH):
                        n = NCH * g + c
                        if n >= 4:
                            pe.wait_ge(ap_evac, n - 3)
                        mm(ps[:, n % 4, 0:CH], poolw[:, g, :], Dp[:, g, c * CH:(c + 1) * CH], start=True, stop=True).then_inc(ap_ready, 1)

                def merge_pool():
                    with pe.Fori(0, KD // 2) as it:
                        for s in range(2):
                            pe.wait_ge(big_in[s], it * 16 + (96 + 16))
                            for c in range(NCH):
                                pe.wait_ge(g_evac, it * 6 + (3 * s + c + 1))
                                slab_chunk(s, c, c, g_ready)
                            pe.wait_ge(small_in[s], it * 16 + 16)
                            for c in range(NCH):
                                pe.wait_ge(p_evac, it * 6 + (3 * s + c + 1))
                                for k in range(4):
                                    last = mm(ps[:, 3 + c, 0:CH], small[:, s, k, :], aP[:, k, c * CH:(c + 1) * CH], start=k == 0, stop=k == 3)
                                last.then_inc(p_ready, 1)

                pe.wait_ge(ap_evac, NG * NCH)
                merge_pool()

                pe.wait_ge(g_evac, 3 + 24)
                pe.wait_ge(p_evac, 3 + 24)
                pe.wait_ge(T_in, 16)

                def logits(n):
                    i, h = divmod(n, NH)
                    t, f = head_tile(h)
                    half = slice(f * HD, (f + 1) * HD)
                    if n >= 2:
                        pe.wait_ge(logit_done, n - 1)
                    for c0 in range(0, lens[i], 512):
                        end = min(c0 + 512, lens[i])
                        bank = 2 * (n % 2) + c0 // 512
                        near = [c for c in (lens[i] - 2 * P, lens[i] - P) if c0 <= c < end]
                        last = mm(ps[:, bank, 0:end - c0], qT[half, t, tile_cols(i)], kT[half, h // 4, c0:end], start=True, stop=not near)
                        for c in near:
                            j = (c - (lens[i] - 2 * P))
                            last = mm(ps[:, bank, c - c0:c - c0 + P], ident[:, :], T[:, h, j:j + P], start=False, stop=c == near[-1])
                    last.then_inc(qk_ready, 1)

                def transpose_probs(n):
                    i = n // NH
                    pe.wait_ge(exp_done, n + 1)
                    for q in range(PTB[i]):
                        b = pt_base(n) + q
                        if b >= 2:
                            pe.wait_ge((pt_evac_a, pt_evac_v)[b % 2], b // 2)
                        for j in range(4 * q, min(4 * q + 4, i + 1)):
                            last = tr(ps[:, 4 + b % 2, j % 4 * P:j % 4 * P + P], lg[:, n % 2, j * P:(j + 1) * P], ident[:, :])
                        last.then_inc(pt_ready, 1)

                def times_values(n):
                    i, h = divmod(n, NH)
                    t, f = head_tile(h)
                    wait_pt_evac(pe, pt_base(n + 1) if n + 1 < UNITS else pt_base(n) + PTB[i])
                    if h == 0 and i:
                        pe.wait_ge(o_evac, i)
                    at = t * P + f * HD
                    for j in range(i + 1):
                        last = mm(ps[:, 6, at:at + HD], PTs[:, n % 2, j * P:(j + 1) * P], vN[:, j, (h // 2) * HD:(h // 2 + 1) * HD],
                                  start=j == 0, stop=j == i)
                    last.then_inc(pv_done, 1)

                def transpose_out(i):
                    pe.wait_ge(o_evac, i + 1)
                    if i:
                        pe.wait_ge(aT_evac, i)
                    for t in range(4):
                        last = tr(ps[:, 7, t * P:(t + 1) * P], onat[:, t * P:(t + 1) * P], ident[:, :])
                    last.then_inc(aT_ready, 1)

                logits(0)
                for n in range(UNITS):
                    if n + 1 < UNITS:
                        logits(n + 1)
                    transpose_probs(n)
                    if n:
                        times_values(n - 1)
                    if n >= NH and n % NH == 1:
                        transpose_out(n // NH - 1)
                times_values(UNITS - 1)
                transpose_out(NBLK - 1)

                pe.wait_ge(logit_done, UNITS)
                wait_pt_evac(pe, pt_base(UNITS - 1) + PTB[-1])
                pe.wait_ge(mask_ready, NBLK - FIRST_TOPK + 1)
                ss_r = ss[:, 0:PAST].rearrange("b (p r) -> b r p", r=KR)
                for rc in range(4):
                    mm(ps[0:64, rc, :], e8[:, :], ss_r[:, 4 * rc:4 * rc + 4, :], start=True, stop=True)
                mm(ps[0:64, 4, 0:1], e8[:, :], ss[:, PAST:PAST + 1], start=True, stop=True).then_inc(sm_ready, 1)
                pe.wait_ge(sm_step, 8)
                pe.wait_ge(aT_evac, NBLK)
                mm(ps[0:NB, 5, 0:64], e8p[:, :], ident[0:64, 0:64], start=True, stop=True)
                for r in range(KR):
                    last = tr(ps[:, 6 + r // 8, r % 8 * 64:r % 8 * 64 + 64], S[:, r * P:(r + 1) * P], ident[0:64, 0:64])
                last.then_inc(sp_ready, 1)
                pe.wait_ge(sp_evac, 1)
                for b in range(NB):
                    pe.wait_ge(v_in[b % 2], 16 * (b // 2 + 1))
                    for g in range(2):
                        out = ps[:, 0, (2 * b + g) * 4:(2 * b + g) * 4 + 4]
                        for r in range(KR):
                            at = r * 256 + g * P
                            mm(out, v_ring[:, b % 2, at:at + P], PT[:, r, 8 * b + 4 * g:8 * b + 4 * g + 4], start=r == 0, stop=False)
                        last = mm(out, vN[0:NB, NBLK, g * P:(g + 1) * P], pd[:, 8 * b + 4 * g:8 * b + 4 * g + 4], start=False, stop=True)
                    last.then_inc(v_used, 1)

            @block.gpsimd
            def _(pool):
                gp = nc.gpsimd
                gp.memset(ident[:, :], 0.0)
                gp.memset(ZI[:, :], 0.0)
                gp.memset(ZQ[:, :, :], 0.0)
                gp.memset(eps[:, :], EPS)
                gp.memset(e8[:, :], 1.0)
                gp.memset(e8t[:, :], 1.0)
                gp.memset(SC[:, 0:offs[FIRST_TOPK]], 0.0)
                gp.memset(U[:, :, 0:16], 0.0)
                gp.memset(R[:, :], 0.0)
                for t in range(15):
                    gp.memset(cfix[:, t:t + 1], 1.0 / (t + 1))
                gp.iota(sub_i[:, :], [[0, 1]], base=0, channel_multiplier=1).then_inc(pool_fill, 1)
                pool.wait_ge(pool_fill, 1)
                gp.affine_select(out=ident[:, :], in_=ident[:, :], compare_op=ALU.not_equal, fill=1.0, base=0,
                                 pattern=[[-1, P]], channel_multiplier=1).then_inc(consts_made, 1)
                gp.affine_select(out=e8[:, :], in_=e8[:, :], compare_op=ALU.is_ge, fill=0.0, base=0,
                                 pattern=[[1, 64]], channel_multiplier=-NH).then_inc(pool_fill, 1)
                gp.affine_select(out=e8t[:, :], in_=e8t[:, :], compare_op=ALU.is_ge, fill=0.0, base=0,
                                 pattern=[[-NH, NB]], channel_multiplier=1).then_inc(pool_fill, 1)
                pool.wait_ge(pool_fill, 3)
                gp.affine_select(out=e8[:, :], in_=e8[:, :], compare_op=ALU.is_ge, fill=0.0, base=NH - 1,
                                 pattern=[[-1, 64]], channel_multiplier=NH).then_inc(consts_made, 1)
                gp.affine_select(out=e8t[:, :], in_=e8t[:, :], compare_op=ALU.is_ge, fill=0.0, base=NH - 1,
                                 pattern=[[NH, NB]], channel_multiplier=-1).then_inc(consts_made, 1)
                for i in range(FIRST_TOPK):
                    d = scs[i][:, i * P:(i + 1) * P]
                    gp.affine_select(out=d, in_=d, compare_op=ALU.is_ge, fill=NEG, base=0, pattern=[[-1, P]],
                                     channel_multiplier=1).then_inc(consts_made, 1)
                pool.wait_ge(consts_in, 16 * N_CONST_DMA)
                starts = bucket_starts()
                for b in range(NBUCKETS):
                    end = starts[b + 1] if b + 1 < NBUCKETS else 256
                    gp.tensor_scalar(R[:, 256 - end:256 - starts[b]], rb[:, b:b + 1].to_broadcast([64, end - starts[b]]),
                                     rb[:, NBUCKETS - 1:NBUCKETS], None, ALU.subtract).then_inc(bias_row, 1)
                pool.wait_ge(bias_row, NBUCKETS)
                pool.dma_start(bias_rows, R[0:NH, :].unsqueeze(1).to_broadcast([NH, P, RW])).then_inc(bias_out, 16)

                pool.wait_ge(rowid_ready, 1)
                for b in range(NB):
                    if b < 2:
                        if b == 0:
                            pool.wait_ge(relu_done, IH * (NBLK - FIRST_TOPK))
                            pool.wait_ge(score_step, IH * (NBLK - FIRST_TOPK))
                    else:
                        pool.wait_ge(kid_used, b - 1)
                    gp.indirect_dma_start(kid[:, b % 2, :], None, i_rows, bass.IndirectOffsetOnAxis(rowid[:, b:b + 1], 0))\
                        .then_inc(kid_in[b % 2], 16)
                    if b == 0:
                        for i in range(FIRST_TOPK, NBLK):
                            pool.wait_ge(score_step, IH * (i - FIRST_TOPK + 1))
                            d = scs[i][:, i * P:(i + 1) * P]
                            gp.affine_select(out=d, in_=d, compare_op=ALU.is_ge, fill=NONCAUSAL, base=0, pattern=[[-1, P]],
                                             channel_multiplier=1).then_inc(causal_done, 1)
                        for f in range(2):
                            gp.tensor_tensor(zw[:, f * 32:(f + 1) * 32].rearrange("b (c h) -> b c h", c=NB),
                                             ident[0:NB, 0:NB].unsqueeze(2).to_broadcast([NB, NB, IH]),
                                             wiN[0:NB, NBLK, :].unsqueeze(1).to_broadcast([NB, NB, IH]), ALU.mult).then_inc(zw_made, 1)

                def load_k(b):
                    if b >= 2:
                        pool.wait_ge(KT_ready, 8 * (b - 1))
                    gp.indirect_dma_start(k_ring[:, b % 2, :], None, k_rows, bass.IndirectOffsetOnAxis(rowid[:, b:b + 1], 0))\
                        .then_inc(k_in[b % 2], 16)

                pool.wait_ge(nat_ready, NT)
                load_k(0)
                load_k(1)

                step = [0]

                def did(ins):
                    step[0] += 1
                    ins.then_inc(mix_step, 1)

                pool.wait_ge(uq_evac, 6 + 12)
                pool.wait_ge(stT_evac, 1)
                pool.wait_ge(sidx_used, NB)
                did(gp.tensor_copy(sx[:, :, :, POOLBUF], U[:, :, 16 + SEQ:16 + TOK]))
                for g in range(NG):
                    w = 2 << g
                    src, lag, b = U[:, g, :], 1, 0
                    while lag < w:
                        lo = 2 * lag - 1
                        if step[0] > 1:
                            pool.wait_ge(mix_step, step[0])
                        did(gp.tensor_tensor(pool_tmp[:, b, lo:16 + SEQ], src[:, lo:16 + SEQ], src[:, lo - lag:16 + SEQ - lag], ALU.add))
                        src, lag, b = pool_tmp[:, b, :], 2 * lag, 1 - b
                    sums = src[:, 16:16 + SEQ]
                    pool.wait_ge(mix_step, step[0])
                    did(gp.tensor_scalar(Dp[:, g, w - 1:SEQ], sums[:, w - 1:SEQ], 1.0 / w, None, ALU.mult))
                    did(gp.tensor_tensor(Dp[:, g, 0:w - 1], sums[:, 0:w - 1], cfix[:, 0:w - 1], ALU.mult))
                    part, lo = w // 2, 16 - w
                    while part:
                        pool.wait_ge(mix_step, step[0])
                        did(gp.tensor_tensor(sx[:, g, :, lo:lo + part], sx[:, g, :, lo:lo + part], sx[:, g, :, lo + part:lo + 2 * part], ALU.add))
                        part //= 2
                    pool.wait_ge(mix_step, step[0])
                    did(gp.tensor_scalar(sd[:, :], sx[:, g, :, lo], 1.0 / w, None, ALU.mult))
                    did(gp.tensor_tensor(Dp[:, g, 0:SEQ], Dp[:, g, 0:SEQ], U[:, g, 16:16 + SEQ], ALU.subtract))
                    pool.wait_ge(mix_step, step[0])
                    gp.tensor_tensor(Dp[:, g, SEQ:TOK], sd[:, :], U[:, g, 16 + SEQ:16 + TOK], ALU.subtract).then_inc(pooled, 1)
                    pool.wait_ge(pooled, g + 1)
                for b in range(2, NB):
                    load_k(b)

                pool.wait_ge(bias_out, 16)
                pool.wait_ge(ap_ready, NG * NCH)
                pool.dma_start(T, bass.AP(bias_rows.tensor, P - 1, [[RW - 1, P], [P * RW, NH], [1, 256]])).then_inc(T_in, 16)

                def load_v(b):
                    if b >= 2:
                        pool.wait_ge(v_used, b - 1)
                    gp.indirect_dma_start(v_ring[:, b % 2, :], None, v_rows, bass.IndirectOffsetOnAxis(rowid[:, b:b + 1], 0))\
                        .then_inc(v_in[b % 2], 16)

                pool.wait_ge(S_ready, 1)
                with pool.Fori(0, KD // 2) as it:
                    for s in range(2):
                        for c in range(NCH):
                            pool.wait_ge(p_evac, it * 6 + (3 + 3 * s + c + 1))
                            gp.tensor_tensor(M[:, bass.ds(it * 2 + s, 1), c * CH:(c + 1) * CH].rearrange("p a c -> p (a c)"),
                                             gbuf[:, s, c, :], pbuf[:, s, c, :], ALU.mult).then_inc(merged, 1)
                load_v(0)
                pool.wait_ge(qk_ready, UNITS)
                for b in range(1, NB):
                    load_v(b)
            @block.scalar
            def _(act):
                A = nc.scalar.activation
                with nc.allow_non_contiguous_dma(reason="small vectors laid out by partition"):
                    act.dma_start(ln1c[:, :], ln1[0].rearrange("(k p) -> p k", p=P)).then_inc(consts_in, 16)
                    act.dma_start(ln2c[:, :], ln2[0].rearrange("(k p) -> p k", p=P)).then_inc(consts_in, 16)
                    act.dma_start(pscl[:, :], pool_scale[0].rearrange("(k p) -> p k", p=P)).then_inc(consts_in, 16)
                    for b in range(NB):
                        act.dma_start(rb[b * NH:(b + 1) * NH, :], rel_bias.rearrange("n h -> h n")).then_inc(consts_in, 16)
                        act.dma_start(pti[:, b:b + 1], bass.AP(page_table.tensor, b * NPAGES, [[1, NPAGES], [0, SR], [1, 1]])).then_inc(consts_in, 16)

                def stats(t):
                    r = rows(t)
                    wait_x(act, t)
                    if t:
                        act.wait_ge(x_squared, t)
                    A(SC[0:r, D:2 * D], x_ring[0:r, t % 3, :], ACT.Square, accum_out=stat[0:r, 0, t:t + 1]).then_inc(x_squared, 1)
                    act.wait_ge(x_squared, t + 1)
                    A(stat[0:r, 1, t:t + 1], stat[0:r, 0, t:t + 1], ACT.Sqrt, bias=eps[0:r, :], scale=1.0 / D).then_inc(x_root, 1)

                def natural_out(t):
                    r, b = rows(t), t % 2
                    act.wait_ge(nat_ready, t + 1)
                    if t >= 2:
                        act.wait_ge(natT_ready, t - 1)
                        act.wait_ge(nat_out[b], 48 * (t // 2))
                    A(kst[0:r, b, 0:256], ps[0:r, 4 + b, 0:256], ACT.Copy)
                    A(vN[0:r, t, :], ps[0:r, 4 + b, 256:512], ACT.Copy)
                    A(kst[0:r, b, 256:512], ps[0:r, 6 + b, 0:256], ACT.Copy)
                    A(kst[0:r, b, 512:640].rearrange("p (f d) -> p f d", f=2),
                      ps[0:r, 6 + b, 256:320].unsqueeze(1).to_broadcast([r, 2, HD]), ACT.Copy)
                    A(wiN[0:r, t, :], ps[0:r, 6 + b, 320:324], ACT.Copy, scale=IH ** -0.5 * HD ** -0.5).then_inc(nat_evac, 1)
                    act.wait_ge(nat_evac, t + 1)
                    dst = [a[tile_cols(t), :] for a in (nk_p, nv_p, ni_p)] if t < NBLK else [nk_s, nv_s, ni_s]
                    act.dma_start(dst[0], kst[0:r, b, 0:256]).then_inc(nat_out[b], 16)
                    act.dma_start(dst[1], vN[0:r, t, :]).then_inc(nat_out[b], 16)
                    act.dma_start(dst[2], kst[0:r, b, 512:576]).then_inc(nat_out[b], 16)

                act.wait_ge(pool_fill, 1)
                stats(0)
                stats(1)
                for t in range(NT):
                    if t + 2 < NT:
                        stats(t + 2)
                    natural_out(t)

                n = 0
                for i in range(FIRST_TOPK, NBLK):
                    for h in range(IH):
                        act.wait_ge(idx_ready, n + 1)
                        if n >= 2:
                            act.wait_ge(score_step, n - 1)
                        A(rl[:, n % 2, 0:lens[i]], flat(4 + 2 * (n % 2))[:, 0:lens[i]], ACT.Relu).then_inc(relu_done, 1)
                        n += 1

                act.wait_ge(nat_evac, NT)
                A(qid, kst[0:NB, 0, 256:512].rearrange("p (h d) -> p h d", h=IH).unsqueeze(2).to_broadcast([NB, IH, 2, HD]),
                  ACT.Copy).then_inc(qid_ready, 1)
                act.wait_ge(zi_ready, 2)
                for f in range(2):
                    half = slice(f * HD, (f + 1) * HD)
                    A(ZI[half, 32 * f:32 * f + NB * (64 + IH)]
                      .rearrange("p (b c) -> p b c", b=NB)[:, :, 0:IH],
                      ps[half, 0, 0:32].rearrange("p (h b) -> p b h", h=IH), ACT.Copy)
                A(wsel[:, :], ps[0:64, 1, 0:NB], ACT.Copy).then_inc(zi_copied, 1)
                act.wait_ge(natT_ready, NT)
                for b in range(2):
                    act.wait_ge(nat_out[b], 48 * len(range(b, NT, 2)))
                for b in range(NB):
                    act.wait_ge(kid_used, b + 1)
                    if b >= 2:
                        act.wait_ge(sidx_used, b - 1)
                    A(kidT[:, b % 2, :], flat(0), ACT.Copy).then_inc(kidT_evac, 1)
                act.wait_ge(sidx_used, NB)
                act.dma_start(poolw, pool_w[0].rearrange("g c e -> c g e")).then_inc(poolw_in, 16)
                A(kid[0:64, 0, :], flat(2)[0:64], ACT.Relu)
                A(rsn[:, :], ps[0:32, 4, 0:1], ACT.Relu).then_inc(sidx_relu, 1)
                act.wait_ge(ssc_ready, 1)
                for f in range(2):
                    A(ss[:, 0:PAST].rearrange("b (p r f) -> b f r p", f=2, p=P)[:, f],
                      flat(4 + 2 * f)[0:NB].rearrange("b (r p) -> b r p", p=P), ACT.Copy)
                A(ss[:, PAST:PAST + 1], ps[0:NB, 0, 0:1], ACT.Copy).then_inc(ss_ready, 1)

                act.sem_inc(uq_evac, 6)
                act.sem_inc(g_evac, 3)
                act.sem_inc(p_evac, 3)
                act.sem_inc(merged, 6)

                with act.Fori(0, U_ITEMS // 2) as it:
                    for s in range(2):
                        for c in range(NCH):
                            act.wait_ge(uq_ready, it * 6 + (3 * s + c + 1))
                            A(U[:, bass.ds(it * 2 + s, 1), 16 + c * CH:16 + (c + 1) * CH].rearrange("p a c -> p (a c)"),
                              ps[:, 3 * s + c, 0:CH], ACT.Copy).then_inc(uq_evac, 1)
                act.wait_ge(stT_ready, 1)
                A(sx[:, :, :, 0:POOLBUF], ps[:, 6, 0:480].rearrange("p (g b t) -> p g b t", g=NG, b=NB), ACT.Copy).then_inc(stT_evac, 1)
                act.wait_ge(uT_ready, 1)
                A(upo[:, :], ps[0:POOLBUF + NB, 7, :], ACT.Copy).then_inc(uT_evac, 1)
                act.wait_ge(uT_evac, 1)
                act.dma_start(new_pool_prompt[0, 0], upo[0:POOLBUF, :]).then_inc(pool_out, 16)
                act.dma_start(new_pool_sample[0, :, POOLBUF - 1, :], upo[POOLBUF:POOLBUF + NB, :]).then_inc(pool_out, 16)
                with act.Fori(0, Q_ITEMS // 2) as it:
                    for s in range(2):
                        for c in range(NCH):
                            act.wait_ge(uq_ready, it * 6 + (12 + 3 * s + c + 1))
                            A(qT[:, bass.ds(it * 2 + s, 1), c * CH:(c + 1) * CH].rearrange("p a c -> p (a c)"),
                              ps[:, 3 * s + c, 0:CH], ACT.Copy, scale=HD ** -0.5).then_inc(uq_evac, 1)
                act.wait_ge(uq_evac, 6 + 24)
                for g in range(2):
                    for f in range(2):
                        half = slice(f * HD, (f + 1) * HD)
                        last = A(ZQ[half, g, :].rearrange("p (b c) -> p b c", b=NB)[:, :, 4 * g + 2 * f:4 * g + 2 * f + 2],
                                 qT[half, 2 * g:2 * g + 2, SEQ:TOK].rearrange("p e b -> p b e"), ACT.Copy)
                last.then_inc(zq_ready, 1)
                for m in range(8 * NB):
                    act.wait_ge(KT_ready, m + 1)
                    if m >= 4:
                        act.wait_ge(KT_used, m - 3)
                    A(KT[:, m % 4, :], ps[:, m % 2, :], ACT.Copy).then_inc(KT_evac, 1)
                act.wait_ge(S_ready, 1)
                A(S[:, 0:PAST], flat(4, 4)[0:64], ACT.Copy)
                A(S[:, PAST:PAST + 1], ps[0:64, 2, 0:1], ACT.Copy).then_inc(S_evac, 1)
                for n in range(NG * NCH):
                    g, c = divmod(n, NCH)
                    act.wait_ge(ap_ready, n + 1)
                    if n == 0:
                        act.wait_ge(pooled, NG)
                    A(aP[:, g, c * CH:(c + 1) * CH], ps[:, n % 4, 0:CH], ACT.Copy, scale=pscl[:, g:g + 1]).then_inc(ap_evac, 1)

                with act.Fori(0, KD // 2) as it:
                    for s in range(2):
                        for c in range(NCH):
                            act.wait_ge(g_ready, it * 6 + (3 * s + c + 1))
                            act.wait_ge(merged, it * 6 + (3 * s + c + 1))
                            A(gbuf[:, s, c, :], ps[:, c, 0:CH], ACT.Sigmoid).then_inc(g_evac, 1)
                        for c in range(NCH):
                            act.wait_ge(p_ready, it * 6 + (3 * s + c + 1))
                            A(pbuf[:, s, c, :], ps[:, 3 + c, 0:CH], ACT.Copy).then_inc(p_evac, 1)

                act.wait_ge(merged, 6 + 24)
                for n in range(UNITS):
                    i, h = divmod(n, NH)
                    t, f = head_tile(h)
                    act.wait_ge(negmax, n + 1)
                    if h == 0 and i >= 2:
                        act.wait_ge(ri_ready, i - 1)
                    A(lg[:, n % 2, 0:lens[i]], lg[:, n % 2, 0:lens[i]], ACT.Exp, bias=mx[:, n % 2, 1:2],
                      accum_out=rs[:, i % 2, 2 * t + f:2 * t + f + 1]).then_inc(exp_done, 1)
                    for q in range(PTB[i]):
                        b = pt_base(n) + q
                        if b % 2:
                            continue
                        act.wait_ge(pt_ready, b + 1)
                        if n >= 2:
                            act.wait_ge(pv_done, n - 1)
                        w = min(4, i + 1 - 4 * q) * P
                        A(PTs[:, n % 2, q * 512:q * 512 + w], ps[:, 4, 0:w], ACT.Copy).then_inc(pt_evac_a, 1)
                    if n >= NH and n % NH == 1:
                        blk = n // NH - 1
                        act.wait_ge(aT_ready, blk + 1)
                        A(qT[:, :, tile_cols(blk)], ps[:, 7, :].rearrange("p (t n) -> p t n", t=4), ACT.Copy).then_inc(aT_evac, 1)
                act.wait_ge(aT_ready, NBLK)
                A(qT[:, :, tile_cols(NBLK - 1)], ps[:, 7, :].rearrange("p (t n) -> p t n", t=4), ACT.Copy).then_inc(aT_evac, 1)

                act.wait_ge(sm_step, 5)
                A(S[:, :], S[:, :], ACT.Exp, bias=smx[:, 1:2], accum_out=smx[:, 2:3]).then_inc(sm_exp, 1)
                act.wait_ge(sp_ready, 1)
                A(pd[:, :], ps[0:NB, 5, 0:64], ACT.Copy)
                A(PT[:, :, :].rearrange("p r n -> p (r n)"), flat(6), ACT.Copy).then_inc(sp_evac, 1)
                act.wait_ge(v_used, NB)
                for f in range(2):
                    half = slice(f * HD, (f + 1) * HD)
                    for g in range(2):
                        last = A(qT[half, 2 * g:2 * g + 2, SEQ:TOK],
                                 ps[half, 0, 0:64].rearrange("p (b g f e) -> p g f e b", b=NB, g=2, f=2)[:, g, f], ACT.Copy)
                last.then_inc(so_evac, 1)


            @block.vector
            def _(dve):
                V = nc.vector

                def scale_x(t):
                    r = rows(t)
                    dve.wait_ge(x_root, t + 1)
                    V.reciprocal(stat[0:r, 2, t:t + 1], stat[0:r, 1, t:t + 1]).then_inc(rstd_ready, 1)
                    dve.wait_ge(rstd_ready, t + 1)
                    V.tensor_scalar(x_ring[0:r, t % 3, :], x_ring[0:r, t % 3, :], stat[0:r, 2, t:t + 1], None, ALU.mult).then_inc(x_scaled, 1)

                def hT_out(t):
                    r = rows(t)
                    for b in range(2):
                        dve.wait_ge(xT_ready, 2 * t + b + 1)
                        V.tensor_tensor(hT[:, 4 * b:4 * b + 4, tile_cols(t)], ps[:, b, :].rearrange("p (k n) -> p k n", k=4)[:, :, 0:r],
                                        ln1c[:, 4 * b:4 * b + 4].unsqueeze(2).to_broadcast([P, 4, r]), ALU.mult).then_inc(hT_ready, 1)

                def naturalT_out(t):
                    r = rows(t)
                    dve.wait_ge(natT_ready, t + 1)
                    V.tensor_copy(kT[:, :, tile_cols(t)], ps[:, 2, 0:256].rearrange("p (k n) -> p k n", k=2)[:, :, 0:r])
                    V.tensor_copy(qiT[:, :, tile_cols(t)], ps[:, 2, 256:512].rearrange("p (k n) -> p k n", k=2)[:, :, 0:r])
                    V.tensor_copy(kiT[:, tile_cols(t)], ps[:, 3, 0:r]).then_inc(natT_evac, 1)

                dve.wait_ge(consts_in, 16 * N_CONST_DMA)
                dve.wait_ge(pool_fill, 1)
                V.tensor_scalar(sub_m[:, :], sub_i[:, :], SR - 1, None, ALU.bitwise_and).then_inc(row_calc, 1)
                dve.wait_ge(row_calc, 1)
                V.tensor_copy(sub_f[:, :], sub_m[:, :]).then_inc(row_calc, 1)
                dve.wait_ge(row_calc, 2)
                V.tensor_scalar(rowid[:, :], pti[:, :], float(SR), sub_f[:, :], ALU.mult, ALU.add).then_inc(rowid_ready, 1)

                scale_x(0)
                scale_x(1)
                hT_out(0)
                for t in range(NT):
                    if t + 2 < NT:
                        scale_x(t + 2)
                    if t + 1 < NT:
                        hT_out(t + 1)
                    if t >= 1:
                        naturalT_out(t - 1)
                naturalT_out(NT - 1)

                dve.wait_ge(nat_evac, NT)
                n = 0
                for i in range(FIRST_TOPK, NBLK):
                    for h in range(IH):
                        dve.wait_ge(relu_done, n + 1)
                        src, w = rl[:, n % 2, 0:lens[i]], wiN[:, i, h:h + 1]
                        if h == 0:
                            V.tensor_scalar(scs[i], src, w, None, ALU.mult).then_inc(score_step, 1)
                        else:
                            dve.wait_ge(score_step, n)
                            V.scalar_tensor_tensor(scs[i], src, w, scs[i], ALU.mult, ALU.add).then_inc(score_step, 1)
                        n += 1

                def find(n, sc, r):
                    if n:
                        dve.wait_ge(top_taken, n)
                    V.max(top8[0:r, :], sc).then_inc(top_max, 1)

                def take(n, sc, r):
                    dve.wait_ge(top_max, n + 1)
                    V.match_replace(sc, top8[0:r, :], sc, TAKEN).then_inc(top_taken, 1)

                def to_mask(k, sc):
                    dve.wait_ge(top_taken, (k + 1) * NRND)
                    V.tensor_scalar(sc, sc, TAKEN, NEG, ALU.not_equal, ALU.mult).then_inc(mask_ready, 1)

                for k, i in enumerate(range(FIRST_TOPK, NBLK)):
                    dve.wait_ge(causal_done, k + 1)
                    for n in range(k * NRND, (k + 1) * NRND):
                        find(n, scs[i], P)
                        take(n, scs[i], P)
                    to_mask(k, scs[i])

                N_PROMPT = NBLK - FIRST_TOPK

                def sample_half_round(m):
                    (find, take)[m % 2](N_PROMPT * NRND + m // 2, ss[:, :], NB)

                HALVES_FIRST = 2 * NRND - (UNITS - 3 * NH)
                FIRST_UNIT = 3 * NH - 2
                dve.wait_ge(ss_ready, 1)
                for m in range(HALVES_FIRST):
                    sample_half_round(m)
                dve.wait_ge(mask_ready, N_PROMPT)

                def row_max(n):
                    i = n // NH
                    dve.wait_ge(qk_ready, n + 1)
                    if n >= 2:
                        dve.wait_ge(pt_ready, pt_base(n - 1))
                    if n == 0:
                        dve.wait_ge(merged, 6 + 24)
                    V.tensor_tensor_reduce(lg[:, n % 2, 0:lens[i]], flat(2 * (n % 2))[:, 0:lens[i]], scs[i], 1.0, 3 * NEG,
                                           ALU.add, ALU.max, mx[:, n % 2, 0:1]).then_inc(logit_done, 1)
                    dve.wait_ge(logit_done, n + 1)
                    V.tensor_scalar(mx[:, n % 2, 1:2], mx[:, n % 2, 0:1], -1.0, None, ALU.mult).then_inc(negmax, 1)

                def out_block(i):
                    dve.wait_ge(pv_done, NH * (i + 1))
                    dve.wait_ge(exp_done, NH * (i + 1))
                    V.reciprocal(ri[:, :], rs[:, i % 2, :]).then_inc(ri_ready, 1)
                    dve.wait_ge(ri_ready, i + 1)
                    if i:
                        dve.wait_ge(aT_ready, i)
                    V.tensor_tensor(onat[:, :].rearrange("p (h d) -> p h d", h=NH), ps[:, 6, :].rearrange("p (h d) -> p h d", h=NH),
                                    ri[:, :].unsqueeze(2).to_broadcast([P, NH, HD]), ALU.mult).then_inc(o_evac, 1)

                row_max(0)
                for n in range(UNITS):
                    i = n // NH
                    if n + 1 < UNITS:
                        row_max(n + 1)
                    if 0 <= n - FIRST_UNIT < 2 * NRND - HALVES_FIRST:
                        sample_half_round(n - FIRST_UNIT + HALVES_FIRST)
                    for q in range(PTB[i]):
                        b = pt_base(n) + q
                        if b % 2 == 0:
                            continue
                        dve.wait_ge(pt_ready, b + 1)
                        if n >= 2:
                            dve.wait_ge(pv_done, n - 1)
                        w = min(4, i + 1 - 4 * q) * P
                        V.tensor_copy(PTs[:, n % 2, q * 512:q * 512 + w], ps[:, 5, 0:w]).then_inc(pt_evac_v, 1)
                    if n >= NH and n % NH == 0:
                        out_block(n // NH - 1)
                to_mask(N_PROMPT, ss[:, :])
                out_block(NBLK - 1)

                dve.wait_ge(sm_ready, 1)
                dve.wait_ge(S_evac, 1)
                V.tensor_tensor(S[:, 0:PAST], S[:, 0:PAST], flat(0, 4)[0:64], ALU.add).then_inc(sm_step, 1)
                dve.wait_ge(bias_row, NBUCKETS)
                V.scalar_tensor_tensor(S[:, PAST:PAST + 1], S[:, PAST:PAST + 1], R[:, 255:256], ps[0:64, 4, 0:1],
                                       ALU.add, ALU.add).then_inc(sm_step, 1)
                dve.wait_ge(sm_step, 2)
                near = S[:, 0:PAST].rearrange("k (r p) -> k r p", p=P)[:, :, P - P // KR:P]
                V.tensor_tensor(near, near, R[:, P - 1:P - 1 + P].rearrange("k (p r) -> k r p", r=KR), ALU.add).then_inc(sm_step, 1)
                dve.wait_ge(sm_step, 3)
                V.tensor_reduce(smx[:, 0:1], S[:, :], AX.X, ALU.max).then_inc(sm_step, 1)
                dve.wait_ge(sm_step, 4)
                V.tensor_scalar(smx[:, 1:2], smx[:, 0:1], -1.0, None, ALU.mult).then_inc(sm_step, 1)
                dve.wait_ge(sm_exp, 1)
                V.reciprocal(smx[:, 3:4], smx[:, 2:3]).then_inc(sm_step, 1)
                dve.wait_ge(sm_step, 6)
                V.tensor_scalar(S[:, :], S[:, :], smx[:, 3:4], None, ALU.mult).then_inc(sm_step, 1)
                dve.wait_ge(sm_step, 7)
                dve.wait_ge(consts_made, 3)
                V.tensor_scalar(e8p[:, :], e8t[:, :], S[:, PAST:PAST + 1], None, ALU.mult).then_inc(sm_step, 1)

        with ExitStack() as ctx:
            def sb(name, shape, dt=F32):
                return sb_in(ctx, name, shape, dt)

            def sem(name):
                return sem_in(ctx, name)

            XH, XL = sb("XH", [P, KD, TOK], F32R), sb("XL", [P, KD, TOK], F32R)
            X_ = {"hi": XH, "lo": XL}
            raw = sb("raw", [P, 2, KD * P])
            sH, sL = sb("sH", [P, 2, KD * P], F32R), sb("sL", [P, 2, KD * P], F32R)
            S_ = {"hi": sH, "lo": sL}
            ap_w = sb("ap_w", [P, 2, 4, P])
            x_nat = sb("x_nat", [P, 2, D])
            gates = sb("gates", [P, NCH, CH])
            gated = sb("gated", [P, NCH, CH])

            x_hi = sem("x_hi"); x_split = sem("x_split"); m_hi = sem("m_hi"); m_split = sem("m_split")
            slab_in = [sem(f"slab_in{b}") for b in range(2)]; slab_hi = sem("slab_hi"); slab_split = sem("slab_split")
            apw_in = [sem(f"apw_in{b}") for b in range(2)]; xn_in = [sem(f"xn_in{b}") for b in range(2)]
            gate_ready = sem("gate2_ready"); gate_done = sem("gate_done"); proj_ready = sem("proj_ready"); gated_done = sem("gated_done"); merge_done = sem("merge_done")
            xt_ready = sem("xt_ready"); xt_done = sem("xt_done"); out_ready = sem("out_ready"); res_done = sem("res_done")

            block = ctx.enter_context(nc.Block())

            @block.sync
            def _(sp):
                def slab(i):
                    if i >= 2:
                        sp.wait_ge(slab_split, i - 1)
                    m = i % KD
                    src = w_in_t[:, :, C_G + D + m * P:C_G + D + (m + 1) * P] if i < KD else wo_t[:, :, m * P:(m + 1) * P]
                    sp.dma_start(raw[:, i % 2].rearrange("p (k n) -> p k n", k=KD), src).then_inc(slab_in[i % 2], 16)

                slab(0)
                slab(1)
                for m in range(KD):
                    if m >= 2:
                        sp.wait_ge(proj_ready, 3 * (m - 1))
                    for f in range(2):
                        for g in range(2):
                            for e in range(2):
                                sp.dma_start(ap_w[f * HD:(f + 1) * HD, m % 2, 2 * g + e, :],
                                             wap_t[f, g, :, e, m * P:(m + 1) * P]).then_inc(apw_in[m % 2], 16)
                    if m >= 2:
                        sp.wait_ge(xt_ready, m - 1)
                    sp.dma_start(x_nat[:, m % 2, :], xp[tile_cols(m), :]).then_inc(xn_in[m % 2], 16)
                    slab(m + 2)
                sp.wait_ge(xt_ready, NBLK - 1)
                sp.dma_start(x_nat[0:NB, 0, :], xs).then_inc(xn_in[0], 16)
                for i in range(KD + 2, 2 * KD):
                    slab(i)

            @block.tensor
            def _(pe):
                mm, tr = nc.tensor.matmul, nc.tensor.transpose

                def transpose_x(r, b):
                    for k in range(KD):
                        last = tr(ps[:, 6 + k // 4, k % 4 * P:k % 4 * P + r], x_nat[0:r, b, k * P:(k + 1) * P], ident[0:r, 0:r])
                    last.then_inc(xt_ready, 1)

                with pe.Fori(0, KD // 2) as it:
                    for s in range(2):
                        pe.wait_ge(slab_split, it * 2 + (s + 1))
                        for c in range(NCH):
                            if s == 0:
                                pe.wait_ge(x_split, KD * (c + 1))
                            pe.wait_ge(gate_done, it * 6 + (3 * s + c + 1))
                            product(ps[:, c, 0:CH], lambda w, k: S_[w][:, s, k * P:(k + 1) * P],
                                    lambda x, k: X_[x][:, k, chunk(c)], KD).then_inc(gate_ready, 1)
                        pe.wait_ge(apw_in[s], it * 128 + 128)
                        for c in range(NCH):
                            pe.wait_ge(gated_done, it * 6 + (3 * s + c + 1))
                            for k in range(4):
                                last = mm(ps[:, 3 + c, 0:CH], ap_w[:, s, k, :], qT[:, k, chunk(c)], start=k == 0, stop=k == 3)
                            last.then_inc(proj_ready, 1)
                        pe.wait_ge(xn_in[s], it * 16 + 16)
                        pe.wait_ge(xt_done, it * 2 + (s + 1))
                        transpose_x(P, s)
                pe.wait_ge(xn_in[0], 16 * (KD // 2 + 1))
                pe.wait_ge(xt_done, KD + 1)
                transpose_x(NB, 0)

                pe.wait_ge(gated_done, 3 + KD * NCH)
                with pe.Fori(0, KD // 2) as it:
                    for s in range(2):
                        pe.wait_ge(slab_split, it * 2 + (KD + s + 1))
                        for c in range(NCH):
                            if s == 0:
                                pe.wait_ge(m_split, KD * (c + 1))
                            pe.wait_ge(res_done, it * 6 + (3 * s + c + 1))
                            product(ps[:, 3 * s + c, 0:CH], lambda w, k: S_[w][:, s, k * P:(k + 1) * P],
                                    lambda x, k: X_[x][:, k, chunk(c)], KD).then_inc(out_ready, 1)

            @block.scalar
            def _(act):
                A = nc.scalar.activation
                order = [(c, k) for c in range(NCH) for k in range(KD)]

                def high_slab(s, count, used=None):
                    act.wait_ge(slab_in[s], count)
                    if used is not None:
                        act.wait_ge(*used)
                    A(sH[:, s, :], raw[:, s, :], ACT.Copy).then_inc(slab_hi, 1)

                act.sem_inc(gate_done, 3)
                act.sem_inc(xt_done, 1)
                high_slab(0, 16)
                for n, (c, k) in enumerate(order):
                    A(XH[:, k, chunk(c)], hT[:, k, chunk(c)], ACT.Copy).then_inc(x_hi, 1)
                    if n == KD:
                        high_slab(1, 16)
                act.wait_ge(x_split, KD * NCH)
                with act.Fori(0, KD // 2) as it:
                    for s in range(2):
                        for c in range(NCH):
                            act.wait_ge(gate_ready, it * 6 + (3 * s + c + 1))
                            act.wait_ge(gated_done, it * 6 + (3 * s + c + 1))
                            A(gates[:, c, :], ps[:, c, 0:CH], ACT.Sigmoid).then_inc(gate_done, 1)
                        high_slab(s, it * 16 + 32)
                        act.wait_ge(xt_ready, it * 2 + (s + 1))
                        A(hT[:, :, bass.ds(it * (2 * P) + s * P, P)], ps[:, 6:8, :].rearrange("p b (k n) -> p (b k) n", k=4), ACT.Copy).then_inc(xt_done, 1)
                act.wait_ge(xt_ready, NT)
                A(hT[:, :, SEQ:TOK], ps[:, 6:8, :].rearrange("p b (k n) -> p (b k) n", k=4)[:, :, 0:NB], ACT.Copy).then_inc(xt_done, 1)
                for n, (c, k) in enumerate(order):
                    act.wait_ge(merge_done, 3 + NCH * (KD - 1) + c + 1)
                    A(XH[:, k, chunk(c)], M[:, k, chunk(c)], ACT.Copy).then_inc(m_hi, 1)
                for i in range(KD + 2, 2 * KD):
                    high_slab(i % 2, 16 * (i // 2 + 1), (out_ready, NCH * (i - KD - 1)))

            @block.gpsimd
            def _(pool):
                gp = nc.gpsimd
                order = [(c, k) for c in range(NCH) for k in range(KD)]

                def low_slab(s, count):
                    pool.wait_ge(slab_hi, count)
                    gp.tensor_tensor(sL[:, s, :], raw[:, s, :], f32(sH[:, s, :]), ALU.subtract).then_inc(slab_split, 1)

                low_slab(0, 1)
                for n, (c, k) in enumerate(order):
                    pool.wait_ge(x_hi, n + 1)
                    gp.tensor_tensor(XL[:, k, chunk(c)], hT[:, k, chunk(c)], f32(XH[:, k, chunk(c)]), ALU.subtract).then_inc(x_split, 1)
                    if n == KD:
                        low_slab(1, 2)
                with pool.Fori(0, KD // 2) as it:
                    for s in range(2):
                        for c in range(NCH):
                            pool.wait_ge(gated_done, it * 6 + (3 + 3 * s + c + 1))
                            m = M[:, bass.ds(it * 2 + s, 1), chunk(c)].rearrange("p a c -> p (a c)")
                            gp.tensor_tensor(m, m, gated[:, c, :], ALU.add).then_inc(merge_done, 1)
                        low_slab(s, it * 2 + (s + 3))
                for n, (c, k) in enumerate(order):
                    pool.wait_ge(m_hi, n + 1)
                    gp.tensor_tensor(XL[:, k, chunk(c)], M[:, k, chunk(c)], f32(XH[:, k, chunk(c)]), ALU.subtract).then_inc(m_split, 1)
                for i in range(KD + 2, 2 * KD):
                    low_slab(i % 2, i + 1)

            @block.vector
            def _(dve):
                V = nc.vector
                dve.sem_inc(gated_done, 3)
                dve.sem_inc(res_done, 6)
                dve.sem_inc(merge_done, 3)
                with dve.Fori(0, KD // 2) as it:
                    for s in range(2):
                        for c in range(NCH):
                            dve.wait_ge(proj_ready, it * 6 + (3 * s + c + 1))
                            dve.wait_ge(gate_done, it * 6 + (3 + 3 * s + c + 1))
                            dve.wait_ge(merge_done, it * 6 + (3 * s + c + 1))
                            V.tensor_tensor(gated[:, c, :], ps[:, 3 + c, 0:CH], gates[:, c, :], ALU.mult).then_inc(gated_done, 1)
                dve.wait_ge(xt_done, 1 + NT)
                with dve.Fori(0, KD // 2) as it:
                    for s in range(2):
                        for c in range(NCH):
                            dve.wait_ge(out_ready, it * 6 + (3 * s + c + 1))
                            m = hT[:, bass.ds(it * 2 + s, 1), chunk(c)].rearrange("p a c -> p (a c)")
                            V.tensor_tensor(m, m, ps[:, 3 * s + c, 0:CH], ALU.add).then_inc(res_done, 1)

        middle.close()

        with ExitStack() as ctx:
            def sb(name, shape, dt=F32):
                return sb_in(ctx, name, shape, dt)

            def sem(name):
                return sem_in(ctx, name)

            hnH, hnL = sb("hnH", [P, KD, TOK], F32R), sb("hnL", [P, KD, TOK], F32R)
            aH, aL = sb("aH", [P, 2, TOK], F32R), sb("aL", [P, 2, TOK], F32R)
            w_raw = sb("w_raw", [P, 3, 2 * KD * P])
            wH, wL = sb("wH", [P, 3, 2 * KD * P], F32R), sb("wL", [P, 3, 2 * KD * P], F32R)
            TMP = sb("TMP", [P, 4 * D])
            sq = TMP[:, 0:4 * CH].rearrange("p (b n) -> p b n", b=4)
            root = TMP[:, 4 * CH:7 * CH].rearrange("p (c n) -> p c n", c=NCH)
            rinv = TMP[:, 7 * CH:10 * CH].rearrange("p (c n) -> p c n", c=NCH)
            sg = TMP[:, 0:2 * CH].rearrange("p (b n) -> p b n", b=2)
            ha = TMP[:, 2 * CH:4 * CH].rearrange("p (b n) -> p b n", b=2)
            yo = TMP[:, 0:2 * D].rearrange("p (b n) -> p b n", b=2)
            junk = TMP[:, 2 * D:3 * D]
            lnf = TMP[:, 3 * D:4 * D]
            ones = sb("ones", [P, P])
            fst = sb("fst", [P, 3, NT])

            ones_made = sem("ones_made"); sq_done = sem("sq_done"); sq_used = sem("sq_used")
            root_done = sem("root_done"); rinv_done = sem("rinv_done"); hn_step = sem("hn_step"); hn_hi = sem("hn_hi"); hn_ready = sem("hn_ready")
            w_in_s = [sem(f"w_in{a}") for a in range(3)]; w_hi = sem("w_hi"); w_lo = sem("w_lo")
            gate_ready = sem("gate_ready"); up_ready = sem("up_ready"); silu_done = sem("silu_done"); act_done = sem("act_done")
            act_hi = sem("act_hi"); act_lo = sem("act_lo"); down_ready = sem("down_ready"); y_done = sem("y_done")
            lnf_in = sem("lnf_in"); yT_ready = sem("yT_ready"); fsq = sem("fsq"); froot = sem("froot"); frinv = sem("frinv"); y_ready = sem("y_ready")
            y_out = [sem(f"y_out{b}") for b in range(2)]

            NPAIR = NF // 2
            CPP = 2 * NCH
            YPP = KD * NCH

            block = ctx.enter_context(nc.Block())

            @block.sync
            def _(sp):
                def load_pair(g, src):
                    for a in range(2):
                        sp.dma_start(w_raw[:, a].rearrange("p (k n) -> p k n", k=KD), wgu_t[:, :, src[a]]).then_inc(w_in_s[a], 16)
                    sp.dma_start(w_raw[:, 2].rearrange("p (k n) -> p k n", k=2), wd_t[:, src[2], :]).then_inc(w_in_s[2], 16)

                load_pair(0, [slice(0, 2 * P), slice(DFF, DFF + 2 * P), slice(0, 2)])
                with sp.Fori(1, NPAIR) as g:
                    src = [bass.ds(g * (2 * P), 2 * P), bass.ds(g * (2 * P) + DFF, 2 * P), bass.ds(g * 2, 2)]
                    sp.wait_ge(w_lo, g * 3)
                    load_pair(g, src)
                sp.wait_ge(act_lo, CPP * NPAIR)
                sp.dma_start(lnf, bass.AP(ln_final.tensor, 0, [[0, P], [1, D]])).then_inc(lnf_in, 16)
                for t in range(NT):
                    sp.wait_ge(y_ready, t + 1)
                    dst = y_prompt[0, tile_cols(t), :] if t < NBLK else y_sample.rearrange("b s d -> (b s) d")
                    sp.dma_start(dst, yo[0:rows(t), t % 2, :]).then_inc(y_out[t % 2], 16)
                for b in range(2):
                    sp.wait_ge(y_out[b], 16 * len(range(b, NT, 2)))

            @block.tensor
            def _(pe):
                mm, tr = nc.tensor.matmul, nc.tensor.transpose
                pe.wait_ge(ones_made, 1)
                for n in range(NCH * KD):
                    c, k = divmod(n, KD)
                    pe.wait_ge(sq_done, n + 1)
                    mm(ps[:, c, 0:CH], ones[:, :], sq[:, n % 4, :], start=k == 0, stop=k == KD - 1).then_inc(sq_used, 1)

                W_ = {"hi": wH, "lo": wL}
                HN = {"hi": hnH, "lo": hnL}
                A_ = {"hi": aH, "lo": aL}
                pe.wait_ge(root_done, NCH)
                with pe.Fori(0, NPAIR) as g:
                    for f in range(2):
                        for c in range(NCH):
                            n = NCH * f + c
                            for a, done, out in ((0, silu_done, gate_ready), (1, act_done, up_ready)):
                                if n == 0:
                                    pe.wait_ge(w_lo, g * 3 + (a + 1))
                                if f == 0 and a == 0:
                                    pe.wait_ge(hn_ready, KD * (c + 1))
                                pe.wait_ge(done, g * CPP + (n + 1))
                                product(ps[:, 2 * (n % 2) + a, 0:CH],
                                        lambda w, k: W_[w][:, a, k * 2 * P + f * P:k * 2 * P + (f + 1) * P],
                                        lambda x, k: HN[x][:, k, chunk(c)], KD).then_inc(out, 1)
                    pe.wait_ge(w_lo, g * 3 + 3)
                    for c in range(NCH):
                        pe.wait_ge(act_lo, g * CPP + (NCH + c + 1))
                        for m in range(KD):
                            n = KD * c + m
                            pe.wait_ge(y_done, g * YPP + (n + 1))
                            product(ps[:, 4 + n % 4, 0:CH], lambda w, k: W_[w][:, 2, k * D + m * P:k * D + (m + 1) * P],
                                    lambda x, k: A_[x][:, k, chunk(c)], 2).then_inc(down_ready, 1)
                pe.wait_ge(y_done, 4 + YPP * NPAIR)
                for t in range(NT):
                    r = rows(t)
                    if t >= 4:
                        pe.wait_ge(y_ready, t - 3)
                    for k in range(KD):
                        last = tr(ps[0:r, 2 * (t % 4) + k // 4, k % 4 * P:k % 4 * P + P], hT[:, k, tile_cols(t)], ident[:, :])
                    last.then_inc(yT_ready, 1)

            @block.gpsimd
            def _(pool):
                gp = nc.gpsimd
                gp.memset(ones[:, :], 1.0).then_inc(ones_made, 1)

                def low_weights(g, parts):
                    for a in parts:
                        pool.wait_ge(w_hi, g * 3 + (a + 1))
                        gp.tensor_tensor(wL[:, a, :], w_raw[:, a, :], f32(wH[:, a, :]), ALU.subtract).then_inc(w_lo, 1)

                def low_activations(g):
                    for n in range(CPP):
                        f, c = divmod(n, NCH)
                        pool.wait_ge(act_hi, g * CPP + (n + 1))
                        gp.tensor_tensor(aL[:, f, chunk(c)], ha[:, n % 2, :], f32(aH[:, f, chunk(c)]), ALU.subtract).then_inc(act_lo, 1)

                low_weights(0, range(3))
                for n in range(NCH * KD):
                    c, k = divmod(n, KD)
                    pool.wait_ge(hn_hi, n + 1)
                    gp.tensor_tensor(hnL[:, k, chunk(c)], sq[:, n % 4, :], f32(hnH[:, k, chunk(c)]), ALU.subtract).then_inc(hn_ready, 1)
                with pool.Fori(0, NPAIR - 1) as g:
                    low_activations(g)
                    low_weights(g + 1, range(3))
                low_activations(NPAIR - 1)

            @block.scalar
            def _(act):
                A = nc.scalar.activation

                def high_weights(g, parts):
                    for a in parts:
                        act.wait_ge(w_in_s[a], g * 16 + 16)
                        A(wH[:, a, :], w_raw[:, a, :], ACT.Copy).then_inc(w_hi, 1)

                def activations(g):
                    for n in range(CPP):
                        f, c = divmod(n, NCH)
                        act.wait_ge(gate_ready, g * CPP + (n + 1))
                        act.wait_ge(act_done, g * CPP + (n + 1))
                        A(sg[:, n % 2, :], ps[:, 2 * (n % 2), 0:CH], ACT.Silu).then_inc(silu_done, 1)
                        act.wait_ge(act_done, g * CPP + (n + 3))
                        A(aH[:, f, chunk(c)], ha[:, n % 2, :], ACT.Copy).then_inc(act_hi, 1)

                for n in range(NCH * KD):
                    c, k = divmod(n, KD)
                    if n >= 4:
                        act.wait_ge(sq_used, n - 3)
                    A(sq[:, n % 4, :], hT[:, k, chunk(c)], ACT.Square).then_inc(sq_done, 1)
                for c in range(NCH):
                    act.wait_ge(sq_used, KD * (c + 1))
                    A(root[:, c, :], ps[:, c, 0:CH], ACT.Sqrt, bias=eps[:, :], scale=1.0 / D).then_inc(root_done, 1)
                act.sem_inc(silu_done, 2)
                high_weights(0, range(3))
                for n in range(NCH * KD):
                    c, k = divmod(n, KD)
                    act.wait_ge(hn_step, n + 1)
                    A(hnH[:, k, chunk(c)], sq[:, n % 4, :], ACT.Copy).then_inc(hn_hi, 1)
                act.wait_ge(hn_ready, NCH * KD)
                with act.Fori(0, NPAIR - 1) as g:
                    activations(g)
                    act.wait_ge(up_ready, g * CPP + CPP)
                    high_weights(g + 1, range(2))
                    act.wait_ge(down_ready, g * YPP + YPP)
                    high_weights(g + 1, (2,))
                activations(NPAIR - 1)
                for t in range(NT):
                    r = rows(t)
                    act.wait_ge(yT_ready, t + 1)
                    if t:
                        act.wait_ge(fsq, t)
                    A(junk[0:r, :], flat(2 * (t % 4))[0:r], ACT.Square, accum_out=fst[0:r, 0, t:t + 1]).then_inc(fsq, 1)
                    act.wait_ge(fsq, t + 1)
                    A(fst[0:r, 1, t:t + 1], fst[0:r, 0, t:t + 1], ACT.Sqrt, bias=eps[0:r, :], scale=1.0 / D).then_inc(froot, 1)

            @block.vector
            def _(dve):
                V = nc.vector
                dve.sem_inc(act_done, 2)
                dve.sem_inc(y_done, 4)
                dve.wait_ge(root_done, NCH)
                for c in range(NCH):
                    V.reciprocal(rinv[:, c, :], root[:, c, :]).then_inc(rinv_done, 1)
                    dve.wait_ge(rinv_done, c + 1)
                    for k in range(KD):
                        n = KD * c + k
                        if n >= 4:
                            dve.wait_ge(hn_ready, n - 3)
                        V.scalar_tensor_tensor(sq[:, n % 4, :], hT[:, k, chunk(c)], ln2c[:, k:k + 1], rinv[:, c, :],
                                               ALU.mult, ALU.mult).then_inc(hn_step, 1)

                with dve.Fori(0, NPAIR) as g:
                    for n in range(CPP):
                        f, c = divmod(n, NCH)
                        dve.wait_ge(silu_done, g * CPP + (n + 3))
                        dve.wait_ge(up_ready, g * CPP + (n + 1))
                        if n >= 2:
                            dve.wait_ge(act_lo, g * CPP + (n - 1))
                        V.tensor_tensor(ha[:, n % 2, :], ps[:, 2 * (n % 2) + 1, 0:CH], sg[:, n % 2, :], ALU.mult).then_inc(act_done, 1)
                    for n in range(YPP):
                        c, m = divmod(n, KD)
                        dve.wait_ge(down_ready, g * YPP + (n + 1))
                        V.tensor_tensor(hT[:, m, chunk(c)], hT[:, m, chunk(c)], ps[:, 4 + n % 4, 0:CH], ALU.add).then_inc(y_done, 1)
                dve.wait_ge(lnf_in, 16)
                for t in range(NT):
                    r = rows(t)
                    dve.wait_ge(froot, t + 1)
                    V.reciprocal(fst[0:r, 2, t:t + 1], fst[0:r, 1, t:t + 1]).then_inc(frinv, 1)
                    dve.wait_ge(frinv, t + 1)
                    if t >= 2:
                        dve.wait_ge(y_out[t % 2], 16 * (t // 2))
                    V.scalar_tensor_tensor(yo[0:r, t % 2, :], flat(2 * (t % 4))[0:r], fst[0:r, 2, t:t + 1], lnf[0:r, :],
                                           ALU.mult, ALU.mult).then_inc(y_ready, 1)


_INS = ["x_prompt", "x_sample", "cache_k", "cache_v", "cache_idx_k", "state_pool", "page_table", "ln1", "w_in", "pool_w",
        "pool_scale", "w_pool_proj", "w_attn_proj", "w_out", "ln2", "w_gate_up", "w_down", "rel_bias", "ln_final"]
_OUTS = [(1, SEQ, D), (NB, 1, D), (1, 1, SEQ, NKV, HD), (1, 1, SEQ, NKV, HD), (1, 1, SEQ, HD), (1, 1, POOLBUF, PW),
         (1, NB, 1, NKV, HD), (1, NB, 1, NKV, HD), (1, NB, 1, HD), (1, NB, POOLBUF, PW)]


def kernel(**inputs):
    import numpy as _np
    import concourse.bacc as _bacc
    from concourse.bass_utils import run_bass_kernel_spmd as _run

    nc = _bacc.Bacc("TRN2", target_bir_lowering=False, num_devices=1)
    arrays, args = {}, []
    for name in _INS:
        a = _np.ascontiguousarray(inputs[name])
        arrays[f"in_{name}_dram"] = a
        args.append(nc.dram_tensor(f"in_{name}_dram", a.shape, mybir.dt.from_np(a.dtype), kind="ExternalInput").ap())
    for i, shape in enumerate(_OUTS):
        args.append(nc.dram_tensor(f"out_{i}_dram", shape, F32, kind="ExternalOutput").ap())
    decoder_layer(nc, *args)
    r = _run(nc, [arrays], core_ids=[0])
    return tuple(r.results[0][f"out_{i}_dram"] for i in range(len(_OUTS)))
```
